# Optimizing a Trainium2 kernel written in Bass

```python
import numpy as np
import jax, jax.numpy as jnp
from jax import lax

D_MODEL = 1024
BATCH = 1
SEQ = 256
DEPTH = 2

HEAD_DIM = 64
ROPE_THETA = 10000.0
RMS_EPS = 1e-6
A_HEADS = 8
A_KV = 1
A_WINDOW = 128
A_QBLOCK = 128
B_HEADS = 8
B_KV = 2
CMP_LEN = 32
CMP_STRIDE = 16
CMP_HIDDEN = 256
SLC_LEN = 64
SLC_TOPN = 8
WIN_LEN = 512
B_QBLOCK = 128
FORCE_BONUS = 1e4
C_HEADS = 16
MOBA_BLOCK = 256
MOBA_TOPK = 3
C_QBLOCK = 32

A_QW = A_HEADS * HEAD_DIM
A_KVW = A_KV * HEAD_DIM
B_QW = B_HEADS * HEAD_DIM
B_KVW = B_KV * HEAD_DIM
B_GATEW = 3 * B_HEADS
C_W = C_HEADS * HEAD_DIM
EVEN_SIZES = (A_QW, A_KVW, A_KVW, A_QW, B_QW, B_KVW, B_KVW, B_KVW, B_KVW, B_KVW, B_KVW, B_GATEW, B_QW)
EVEN_WIDTH = A_QW + 2 * A_KVW + A_QW + B_QW + 6 * B_KVW + B_GATEW + B_QW
EVEN_OUT = A_QW + B_QW
ODD_SIZES = (C_W, C_W, C_W, C_W)
ODD_WIDTH = 4 * C_W
N_EVEN = (DEPTH + 1) // 2
N_ODD = DEPTH // 2


def _offsets(sizes):
    out, acc = [], 0
    for s in sizes[:-1]:
        acc += s
        out.append(acc)
    return out

def rms_norm(x, g):
    xf = x.astype(jnp.float32)
    y = xf * lax.rsqrt(jnp.mean(xf * xf, axis=-1, keepdims=True) + RMS_EPS)
    return (y * g.astype(jnp.float32)).astype(x.dtype)

def rope_tables(n):
    inv = ROPE_THETA ** (-jnp.arange(0, HEAD_DIM, 2, dtype=jnp.float32) / HEAD_DIM)
    ang = jnp.arange(n, dtype=jnp.float32)[:, None] * inv[None, :]
    return jnp.cos(ang), jnp.sin(ang)

def apply_rope(x, cos, sin):
    half = HEAD_DIM // 2
    xf = x.astype(jnp.float32)
    x1, x2 = xf[..., :half], xf[..., half:]
    return jnp.concatenate([x1 * cos - x2 * sin, x2 * cos + x1 * sin], axis=-1).astype(x.dtype)

def split_heads(t, n):
    b, s, _ = t.shape
    return t.reshape(b, s, n, HEAD_DIM).transpose(0, 2, 1, 3)

def merge_heads(o):
    b, h, s, d = o.shape
    return o.transpose(0, 2, 1, 3).reshape(b, s, h * d)

def masked_softmax(s, mask, sink=None):
    s = jnp.where(mask, s, -jnp.inf)
    m = jnp.max(s, axis=-1, keepdims=True)
    if sink is not None:
        m = jnp.maximum(m, sink)
    m = jnp.where(jnp.isfinite(m), m, 0.0)
    e = jnp.where(mask, jnp.exp(s - m), 0.0)
    den = jnp.sum(e, axis=-1, keepdims=True)
    if sink is not None:
        den = den + jnp.exp(sink - m)
    return e / jnp.where(den > 0, den, 1.0)

def gather_blocks(kb, idx):
    return jax.vmap(jax.vmap(lambda a, i: a[i]))(kb, idx)

def banded_attention(q, k, v, window, block, sink=None):
    b, g, r, s, d = q.shape
    nb = s // block
    n_prev = -(-(window - 1) // block)
    span = (n_prev + 1) * block
    pad = n_prev * block
    kp = jnp.pad(k, ((0, 0), (0, 0), (pad, 0), (0, 0)))
    vp = jnp.pad(v, ((0, 0), (0, 0), (pad, 0), (0, 0)))
    idx = np.arange(nb)[:, None] * block + np.arange(span)[None, :]
    kb = kp[:, :, idx]
    vb = vp[:, :, idx]
    qb = q.reshape(b, g, r, nb, block, d)
    sc = jnp.einsum('bgrnqd,bgnkd->bgrnqk', qb, kb).astype(jnp.float32) * (HEAD_DIM ** -0.5)
    qpos = np.arange(nb)[:, None] * block + np.arange(block)[None, :]
    kpos = idx - pad
    diff = qpos[:, :, None] - kpos[:, None, :]
    mask = jnp.asarray((diff >= 0) & (diff < window) & (kpos[:, None, :] >= 0))
    sk = None if sink is None else sink.astype(jnp.float32).reshape(1, g, r, 1, 1, 1)
    p = masked_softmax(sc, mask, sk)
    o = jnp.einsum('bgrnqk,bgnkd->bgrnqd', p.astype(v.dtype), vb)
    return o.reshape(b, g, r, s, d)

def swa_sink_attention(qa, ka, va, sinks, cos, sin):
    b, s, _ = qa.shape
    q = apply_rope(split_heads(qa, A_HEADS), cos, sin).reshape(b, A_KV, A_HEADS // A_KV, s, HEAD_DIM)
    k = apply_rope(split_heads(ka, A_KV), cos, sin)
    v = split_heads(va, A_KV)
    o = banded_attention(q, k, v, A_WINDOW, A_QBLOCK, sinks.reshape(A_KV, A_HEADS // A_KV))
    return merge_heads(o.reshape(b, A_HEADS, s, HEAD_DIM))

def compress_mlp(blocks, pe, w1, w2):
    b, g, nc, l, d = blocks.shape
    u = (blocks + pe).reshape(b, g, nc, l * d)
    return jax.nn.gelu(u @ w1) @ w2

def nsa_attention(qb, kc, vc, ks, vs, kw, vw, gl, pe_k, w1k, w2k, pe_v, w1v, w2v, cos, sin):
    b, s, _ = qb.shape
    rr = B_HEADS // B_KV
    scale = HEAD_DIM ** -0.5
    q = apply_rope(split_heads(qb, B_HEADS), cos, sin).reshape(b, B_KV, rr, s, HEAD_DIM)
    kc = apply_rope(split_heads(kc, B_KV), cos, sin)
    ks = apply_rope(split_heads(ks, B_KV), cos, sin)
    kw = apply_rope(split_heads(kw, B_KV), cos, sin)
    vc, vs, vw = split_heads(vc, B_KV), split_heads(vs, B_KV), split_heads(vw, B_KV)

    nc = (s - CMP_LEN) // CMP_STRIDE + 1
    cidx = np.arange(nc)[:, None] * CMP_STRIDE + np.arange(CMP_LEN)[None, :]
    k_cmp = compress_mlp(kc[:, :, cidx], pe_k, w1k, w2k)
    v_cmp = compress_mlp(vc[:, :, cidx], pe_v, w1v, w2v)
    sc = jnp.einsum('bgrsd,bgcd->bgrsc', q, k_cmp).astype(jnp.float32) * scale
    mask_c = jnp.asarray(np.arange(s)[:, None] >= cidx[None, :, -1])
    p_cmp = masked_softmax(sc, mask_c)
    o_cmp = jnp.einsum('bgrsc,bgcd->bgrsd', p_cmp.astype(v_cmp.dtype), v_cmp)

    nsb = s // SLC_LEN
    cst = cidx[:, 0]
    jj = np.arange(nsb)
    overlap = ((cst[:, None] < (jj[None, :] + 1) * SLC_LEN) & (cst[:, None] + CMP_LEN > jj[None, :] * SLC_LEN)).astype(np.float32)
    imp = jnp.einsum('bgrsc,cj->bgsj', p_cmp, jnp.asarray(overlap))
    tb = np.arange(s)[:, None] // SLC_LEN
    valid = jnp.asarray(jj[None, :] <= tb)
    forced = jnp.asarray((jj[None, :] == 0) | (jj[None, :] == tb) | (jj[None, :] == tb - 1))
    score = jnp.where(valid, jnp.where(forced, FORCE_BONUS, imp), -jnp.inf)
    top_s, top_i = lax.top_k(score, min(SLC_TOPN, nsb))
    sel_ok = top_s > -jnp.inf
    n_sel = top_i.shape[-1]
    ksb = ks.reshape(b, B_KV, nsb, SLC_LEN, HEAD_DIM)
    vsb = vs.reshape(b, B_KV, nsb, SLC_LEN, HEAD_DIM)

    def sel_chunk(ci):
        start = ci * B_QBLOCK
        qc = lax.dynamic_slice_in_dim(q, start, B_QBLOCK, axis=3)
        ic = lax.dynamic_slice_in_dim(top_i, start, B_QBLOCK, axis=2)
        okc = lax.dynamic_slice_in_dim(sel_ok, start, B_QBLOCK, axis=2)
        kg = gather_blocks(ksb, ic)
        vg = gather_blocks(vsb, ic)
        sc_ = jnp.einsum('bgrqd,bgqnkd->bgrqnk', qc, kg).astype(jnp.float32) * scale
        tpos = start + jnp.arange(B_QBLOCK)
        kpos = ic[..., None] * SLC_LEN + jnp.arange(SLC_LEN)
        msk = okc[..., None] & (kpos <= tpos[None, None, :, None, None])
        m_tot = n_sel * SLC_LEN
        p = masked_softmax(sc_.reshape(b, B_KV, rr, B_QBLOCK, m_tot), msk.reshape(b, B_KV, 1, B_QBLOCK, m_tot))
        return jnp.einsum('bgrqm,bgqmd->bgrqd', p.astype(vg.dtype), vg.reshape(b, B_KV, B_QBLOCK, m_tot, HEAD_DIM))

    o_slc = lax.map(sel_chunk, jnp.arange(s // B_QBLOCK))
    o_slc = o_slc.transpose(1, 2, 3, 0, 4, 5).reshape(b, B_KV, rr, s, HEAD_DIM)

    o_win = banded_attention(q, kw, vw, WIN_LEN, B_QBLOCK)

    g = jax.nn.sigmoid(gl.astype(jnp.float32)).reshape(b, s, B_KV, rr, 3).transpose(0, 2, 3, 1, 4).astype(q.dtype)
    o = g[..., 0:1] * o_cmp + g[..., 1:2] * o_slc + g[..., 2:3] * o_win
    return merge_heads(o.reshape(b, B_HEADS, s, HEAD_DIM))

def moba_attention(qc_, kc_, vc_, cos, sin):
    b, s, _ = qc_.shape
    scale = HEAD_DIM ** -0.5
    q = apply_rope(split_heads(qc_, C_HEADS), cos, sin)
    k = apply_rope(split_heads(kc_, C_HEADS), cos, sin)
    v = split_heads(vc_, C_HEADS)
    sp = -(-s // MOBA_BLOCK) * MOBA_BLOCK
    padw = ((0, 0), (0, 0), (0, sp - s), (0, 0))
    q, k, v = jnp.pad(q, padw), jnp.pad(k, padw), jnp.pad(v, padw)
    nblk = sp // MOBA_BLOCK
    kb = k.reshape(b, C_HEADS, nblk, MOBA_BLOCK, HEAD_DIM)
    vb = v.reshape(b, C_HEADS, nblk, MOBA_BLOCK, HEAD_DIM)
    kmean = jnp.mean(kb.astype(jnp.float32), axis=3)
    gs = jnp.einsum('bhsd,bhjd->bhsj', q.astype(jnp.float32), kmean)
    past = jnp.asarray(np.arange(nblk)[None, :] < (np.arange(sp) // MOBA_BLOCK)[:, None])
    gs = jnp.where(past, gs, -jnp.inf)
    top_s, top_i = lax.top_k(gs, min(MOBA_TOPK, nblk))
    ok = top_s > -jnp.inf
    n_sel = top_i.shape[-1]

    def chunk(ci):
        start = ci * C_QBLOCK
        qc = lax.dynamic_slice_in_dim(q, start, C_QBLOCK, axis=2)
        ic = lax.dynamic_slice_in_dim(top_i, start, C_QBLOCK, axis=2)
        okc = lax.dynamic_slice_in_dim(ok, start, C_QBLOCK, axis=2)
        kg = gather_blocks(kb, ic)
        vg = gather_blocks(vb, ic)
        s_sel = jnp.einsum('bhqd,bhqnkd->bhqnk', qc, kg).astype(jnp.float32).reshape(b, C_HEADS, C_QBLOCK, n_sel * MOBA_BLOCK)
        own = (start // MOBA_BLOCK) * MOBA_BLOCK
        kown = lax.dynamic_slice_in_dim(k, own, MOBA_BLOCK, axis=2)
        vown = lax.dynamic_slice_in_dim(v, own, MOBA_BLOCK, axis=2)
        s_own = jnp.einsum('bhqd,bhkd->bhqk', qc, kown).astype(jnp.float32)
        tpos = start + jnp.arange(C_QBLOCK)
        m_own = (own + jnp.arange(MOBA_BLOCK))[None, :] <= tpos[:, None]
        m_sel = jnp.repeat(okc, MOBA_BLOCK, axis=-1)
        mask = jnp.concatenate([m_sel, jnp.broadcast_to(m_own, (b, C_HEADS, C_QBLOCK, MOBA_BLOCK))], axis=-1)
        p = masked_softmax(jnp.concatenate([s_sel, s_own], axis=-1) * scale, mask).astype(v.dtype)
        nk = n_sel * MOBA_BLOCK
        o = jnp.einsum('bhqm,bhqmd->bhqd', p[..., :nk], vg.reshape(b, C_HEADS, C_QBLOCK, nk, HEAD_DIM))
        return o + jnp.einsum('bhqk,bhkd->bhqd', p[..., nk:], vown)

    o = lax.map(chunk, jnp.arange(sp // C_QBLOCK))
    o = o.transpose(1, 2, 0, 3, 4).reshape(b, C_HEADS, sp, HEAD_DIM)[:, :, :s]
    return merge_heads(o)

def even_mixer(h, w_in, w_out, sinks, pe_k, w1k, w2k, pe_v, w1v, w2v, cos, sin):
    proj = jnp.einsum('bsd,de->bse', h, w_in)
    qa, ka, va, za, qb, kc, vc, ks, vs, kw, vw, gb, zb = jnp.split(proj, _offsets(EVEN_SIZES), axis=-1)
    oa = swa_sink_attention(qa, ka, va, sinks, cos, sin) * jax.nn.silu(za)
    ob = nsa_attention(qb, kc, vc, ks, vs, kw, vw, gb, pe_k, w1k, w2k, pe_v, w1v, w2v, cos, sin) * jax.nn.silu(zb)
    return jnp.einsum('bse,ed->bsd', jnp.concatenate([oa, ob], axis=-1), w_out)

def odd_mixer(h, w_in, w_out, cos, sin):
    proj = jnp.einsum('bsd,de->bse', h, w_in)
    q, k, v, z = jnp.split(proj, _offsets(ODD_SIZES), axis=-1)
    o = moba_attention(q, k, v, cos, sin) * jax.nn.silu(z)
    return jnp.einsum('bse,ed->bsd', o, w_out)

def first_inputs(seed: int = 0) -> dict:
    key = jax.random.key(seed)
    ks = jax.random.split(key, 20)
    nrm = lambda k, shape, sc: jax.random.normal(k, shape, jnp.float32) * sc
    d = D_MODEL
    fl = CMP_LEN * HEAD_DIM
    return {
        "x": nrm(ks[0], (BATCH, SEQ, d), 1.0),
        "c": nrm(ks[1], (BATCH, d), 1.0),
        "w_ada": nrm(ks[2], (DEPTH, d, 3 * d), 0.5 * d ** -0.5),
        "b_ada": nrm(ks[3], (DEPTH, 3 * d), 0.01),
        "norm_g": 1.0 + nrm(ks[4], (DEPTH, d), 0.02),
        "w_in_even": nrm(ks[5], (N_EVEN, d, EVEN_WIDTH), d ** -0.5),
        "a_sinks": nrm(ks[6], (N_EVEN, A_HEADS), 0.5),
        "cmp_pe_k": nrm(ks[7], (N_EVEN, CMP_LEN, HEAD_DIM), 0.1),
        "cmp_w1_k": nrm(ks[8], (N_EVEN, fl, CMP_HIDDEN), fl ** -0.5),
        "cmp_w2_k": nrm(ks[9], (N_EVEN, CMP_HIDDEN, HEAD_DIM), CMP_HIDDEN ** -0.5),
        "cmp_pe_v": nrm(ks[10], (N_EVEN, CMP_LEN, HEAD_DIM), 0.1),
        "cmp_w1_v": nrm(ks[11], (N_EVEN, fl, CMP_HIDDEN), fl ** -0.5),
        "cmp_w2_v": nrm(ks[12], (N_EVEN, CMP_HIDDEN, HEAD_DIM), CMP_HIDDEN ** -0.5),
        "w_out_even": nrm(ks[13], (N_EVEN, EVEN_OUT, d), EVEN_OUT ** -0.5),
        "w_in_odd": nrm(ks[14], (N_ODD, d, ODD_WIDTH), d ** -0.5),
        "w_out_odd": nrm(ks[15], (N_ODD, C_W, d), C_W ** -0.5),
        "final_g": 1.0 + nrm(ks[16], (d,), 0.02),
    }

def first_block(x, c, w_ada, b_ada, norm_g, w_in_even, a_sinks, cmp_pe_k, cmp_w1_k, cmp_w2_k,
              cmp_pe_v, cmp_w1_v, cmp_w2_v, w_out_even, w_in_odd, w_out_odd, final_g):
    cos, sin = rope_tables(x.shape[1])
    c_act = jax.nn.silu(c)
    for layer in range(DEPTH):
        ada = jnp.einsum('bd,de->be', c_act, w_ada[layer]) + b_ada[layer]
        shift, scale, gate = jnp.split(ada, 3, axis=-1)
        h = rms_norm(x, norm_g[layer]) * (1.0 + scale[:, None, :]) + shift[:, None, :]
        i = layer // 2
        if layer % 2 == 0:
            y = even_mixer(h, w_in_even[i], w_out_even[i], a_sinks[i], cmp_pe_k[i], cmp_w1_k[i], cmp_w2_k[i],
                           cmp_pe_v[i], cmp_w1_v[i], cmp_w2_v[i], cos, sin)
        else:
            y = odd_mixer(h, w_in_odd[i], w_out_odd[i], cos, sin)
        x = x + gate[:, None, :] * y
    return rms_norm(x, final_g)


DEPTH_2 = 1

N_HEADS = 8
W_ATTN = N_HEADS * HEAD_DIM
C_CONF = D_MODEL // 2
CONF_WIDTH = 31
C_SC = D_MODEL // 2
SC_WIDTH = 3
N_BRANCH = 3
D_FF = ((8 * D_MODEL + 2) // 3 + 255) // 256 * 256
BLOCK_Q = 128
EPS = 1e-6
SPLIT_SIZES = (W_ATTN, W_ATTN, W_ATTN, C_CONF, C_CONF, C_SC, C_SC, C_SC, N_BRANCH * D_MODEL)
SPLIT_IDX = tuple(int(i) for i in np.cumsum(SPLIT_SIZES)[:-1])
N_IN = int(sum(SPLIT_SIZES))


def rms_norm_2(x, g):
    xf = x.astype(jnp.float32)
    y = xf * lax.rsqrt(jnp.mean(xf * xf, axis=-1, keepdims=True) + EPS)
    return (y * g.astype(jnp.float32)).astype(x.dtype)

def layer_norm(x, g, b):
    xf = x.astype(jnp.float32)
    mu = jnp.mean(xf, axis=-1, keepdims=True)
    var = jnp.mean(jnp.square(xf - mu), axis=-1, keepdims=True)
    y = (xf - mu) * lax.rsqrt(var + EPS)
    return (y * g.astype(jnp.float32) + b.astype(jnp.float32)).astype(x.dtype)

def causal_depthwise_conv(x, w):
    width, ch = w.shape
    return lax.conv_general_dilated(
        x, w[:, None, :].astype(x.dtype), window_strides=(1,), padding=[(width - 1, 0)],
        dimension_numbers=("NWC", "WIO", "NWC"), feature_group_count=ch)

def stick_breaking_attention(q, k, v):
    b, h, s, dh = q.shape
    nb = s // BLOCK_Q
    scale = float(1.0 / np.sqrt(dh))
    qb = q.reshape(b, h, nb, BLOCK_Q, dh).transpose(2, 0, 1, 3, 4)
    kpos = jnp.arange(s)

    def one_block(args):
        qi, bi = args
        z = jnp.einsum("bhqd,bhkd->bhqk", qi, k, preferred_element_type=jnp.float32) * scale
        qpos = bi * BLOCK_Q + jnp.arange(BLOCK_Q)
        causal = kpos[None, :] < qpos[:, None]
        log_1m_beta = jnp.where(causal, -jax.nn.softplus(z), 0.0)
        rest = lax.cumsum(log_1m_beta, axis=log_1m_beta.ndim - 1, reverse=True) - log_1m_beta
        attn = jnp.where(causal, jnp.exp(jax.nn.log_sigmoid(z) + rest), 0.0)
        return jnp.einsum("bhqk,bhkd->bhqd", attn.astype(v.dtype), v)

    out = lax.map(one_block, (qb, jnp.arange(nb)))
    return out.transpose(1, 2, 0, 3, 4).reshape(b, h, s, dh)

def second_inputs(seed: int = 0) -> dict:
    key = jax.random.key(seed)
    ks = jax.random.split(key, 20)
    f32 = jnp.float32

    def nrm(k, shape, fan_in):
        return jax.random.normal(k, shape, f32) * (fan_in ** -0.5)

    def gain(k, shape):
        return 1.0 + 0.05 * jax.random.normal(k, shape, f32)

    def small(k, shape):
        return 0.02 * jax.random.normal(k, shape, f32)

    L = DEPTH_2
    return {
        "x": jax.random.normal(ks[0], (BATCH, SEQ, D_MODEL), f32),
        "mix_norm_g": gain(ks[1], (L, D_MODEL)),
        "w_in": nrm(ks[2], (L, D_MODEL, N_IN), D_MODEL),
        "q_norm_g": gain(ks[3], (L, HEAD_DIM)),
        "k_norm_g": gain(ks[4], (L, HEAD_DIM)),
        "w_attn_out": nrm(ks[5], (L, W_ATTN, D_MODEL), W_ATTN),
        "conf_dw_w": nrm(ks[6], (L, CONF_WIDTH, C_CONF), CONF_WIDTH),
        "conf_dw_b": small(ks[7], (L, C_CONF)),
        "conf_ln_g": gain(ks[8], (L, C_CONF)),
        "conf_ln_b": small(ks[9], (L, C_CONF)),
        "w_conf_out": nrm(ks[10], (L, C_CONF, D_MODEL), C_CONF),
        "sc_conv_w": nrm(ks[11], (L, SC_WIDTH, C_SC), SC_WIDTH),
        "w_sc_out": nrm(ks[12], (L, C_SC, D_MODEL), C_SC),
        "gate_b": small(ks[13], (L, N_BRANCH, D_MODEL)),
        "w_o": nrm(ks[14], (L, D_MODEL, D_MODEL), D_MODEL),
        "ffn_norm_g": gain(ks[15], (L, D_MODEL)),
        "w_ffn_in": nrm(ks[16], (L, D_MODEL, 2 * D_FF), D_MODEL),
        "w_ffn_out": nrm(ks[17], (L, D_FF, D_MODEL), D_FF),
    }

def second_block(x, mix_norm_g, w_in, q_norm_g, k_norm_g, w_attn_out, conf_dw_w, conf_dw_b,
              conf_ln_g, conf_ln_b, w_conf_out, sc_conv_w, w_sc_out, gate_b, w_o,
              ffn_norm_g, w_ffn_in, w_ffn_out):
    b, s, _ = x.shape
    for l in range(DEPTH_2):
        u = rms_norm_2(x, mix_norm_g[l])
        proj = u @ w_in[l]
        q, k, v, cf_val, cf_gate, sc_x, sc_bg, sc_cg, gates = jnp.split(proj, SPLIT_IDX, axis=-1)

        q = rms_norm_2(q.reshape(b, s, N_HEADS, HEAD_DIM), q_norm_g[l]).transpose(0, 2, 1, 3)
        k = rms_norm_2(k.reshape(b, s, N_HEADS, HEAD_DIM), k_norm_g[l]).transpose(0, 2, 1, 3)
        v = v.reshape(b, s, N_HEADS, HEAD_DIM).transpose(0, 2, 1, 3)
        o = stick_breaking_attention(q, k, v).transpose(0, 2, 1, 3).reshape(b, s, W_ATTN)
        y_a = o @ w_attn_out[l]

        hb = cf_val * jax.nn.sigmoid(cf_gate)
        hb = causal_depthwise_conv(hb, conf_dw_w[l]) + conf_dw_b[l]
        hb = jax.nn.silu(layer_norm(hb, conf_ln_g[l], conf_ln_b[l]))
        y_b = hb @ w_conf_out[l]

        hc = sc_bg * causal_depthwise_conv(sc_cg * sc_x, sc_conv_w[l])
        y_c = hc @ w_sc_out[l]

        g = jax.nn.sigmoid(gates.reshape(b, s, N_BRANCH, D_MODEL) + gate_b[l])
        merged = g[:, :, 0] * y_a + g[:, :, 1] * y_b + g[:, :, 2] * y_c
        x = x + merged @ w_o[l]

        hf = rms_norm_2(x, ffn_norm_g[l]) @ w_ffn_in[l]
        gt, up = jnp.split(hf, 2, axis=-1)
        x = x + (jax.nn.silu(gt) * up) @ w_ffn_out[l]
    return x


def setup_inputs(seed=0):
    out = dict(first_inputs(seed))
    for name, value in second_inputs(seed + 1).items():
        if name != "x":
            out[name + "_2"] = value
    return out


def reference(
    x, c, w_ada, b_ada, norm_g, w_in_even, a_sinks, cmp_pe_k, cmp_w1_k, cmp_w2_k, cmp_pe_v,
    cmp_w1_v, cmp_w2_v, w_out_even, w_in_odd, w_out_odd, final_g, mix_norm_g_2, w_in_2,
    q_norm_g_2, k_norm_g_2, w_attn_out_2, conf_dw_w_2, conf_dw_b_2, conf_ln_g_2, conf_ln_b_2,
    w_conf_out_2, sc_conv_w_2, w_sc_out_2, gate_b_2, w_o_2, ffn_norm_g_2, w_ffn_in_2,
    w_ffn_out_2,
):
    x = first_block(
        x, c, w_ada, b_ada, norm_g, w_in_even, a_sinks, cmp_pe_k, cmp_w1_k, cmp_w2_k, cmp_pe_v,
        cmp_w1_v, cmp_w2_v, w_out_even, w_in_odd, w_out_odd, final_g,
    )
    return second_block(
        x, mix_norm_g_2, w_in_2, q_norm_g_2, k_norm_g_2, w_attn_out_2, conf_dw_w_2, conf_dw_b_2,
        conf_ln_g_2, conf_ln_b_2, w_conf_out_2, sc_conv_w_2, w_sc_out_2, gate_b_2, w_o_2,
        ffn_norm_g_2, w_ffn_in_2, w_ffn_out_2,
    )


_drawn_inputs = setup_inputs


def setup_inputs(seed=0):
    import zlib

    import numpy as np

    out = dict(_drawn_inputs(seed))
    spreads = {}
    factors = {'b_ada': 8.0,
     'norm_g': 8.0,
     'a_sinks': 8.0,
     'cmp_pe_k': 8.0,
     'cmp_w1_k': 3.483,
     'cmp_w2_k': 3.558,
     'cmp_pe_v': 8.0,
     'q_norm_g_2': 7.787,
     'k_norm_g_2': 7.796,
     'conf_dw_b_2': 4.726,
     'conf_ln_g_2': 3.324,
     'conf_ln_b_2': 8.0,
     'gate_b_2': 8.0}
    for name, (base, spread) in spreads.items():
        noise = np.random.default_rng([zlib.crc32(name.encode()), seed]).standard_normal(out[name].shape)
        drawn = base * np.exp(spread * noise) if base else spread * noise
        out[name] = __import__('jax').numpy.asarray(drawn.astype(out[name].dtype))
    for name, factor in factors.items():
        out[name] = (out[name] * factor).astype(out[name].dtype)
    return out
```

```python
from contextlib import ExitStack

import numpy as np

import concourse.bass as bass
from concourse import mybir

F32 = mybir.dt.float32
ALU = mybir.AluOpType
ACT = mybir.ActivationFunctionType
AX = mybir.AxisListType

P = 128
S = 256
NT = S // P
D = 1024
KB = D // P
HD = 64
HALF = HD // 2
EPS = 1e-6
SCALE = HD ** -0.5
NEG = -1e30
A_HEADS, B_HEADS, B_GROUPS, C_HEADS, S_HEADS = 8, 8, 2, 16, 8
CMP_LEN, CMP_STRIDE, CMP_HID = 32, 16, 256
NC = (S - CMP_LEN) // CMP_STRIDE + 1
D_FF = 2816
FB = D_FF // P
CONF_TAPS, SC_TAPS = 31, 3
CB = 4
CHUNK = 4096
RING = 3
TRI = 384


def chunk_table():
    def ada(layer, c):
        return (f"ada{layer}_{c}", KB, 512)

    def plain(*names):
        return [(n, KB, 512) for n in names]

    t = [ada(0, c) for c in range(4)] + plain("kcks") + [ada(0, 4), ("kakw", KB, 408), ada(0, 5)]
    t += plain("qa") + [ada(1, 0)] + plain("qb") + [ada(1, 1), ("w1k", 16, 256), ada(1, 2), ("w1v", 16, 256), ada(1, 3)]
    t += plain("za") + [ada(1, 4)] + plain("zb") + [ada(1, 5)] + plain("wo0_0", "wo0_1")
    for g in range(2):
        t += [(f"{n}1_{g}", KB, 512) for n in "qkvz"]
    t += [("wo1_0", KB, 512), ("wo1_1", KB, 512)]
    t += [(n, KB, 512) for n in ("val", "cga", "q2", "k2", "v2", "scx", "scg", "sbg")]
    t += [(f"g{i}", KB, 512) for i in range(6)]
    t += [("sco", 4, 1024), ("cfo", 4, 1024), ("ato", 4, 1024), ("wf0", KB, 512), ("wf1", KB, 512)]
    t += [(f"fi{i}", KB, 512) for i in range(FB // 2)]
    t += [(f"fo{i}", min(4, FB - 4 * i), 1024) for i in range((FB + 3) // 4)]
    return t


def column_table():
    sizes = [("c", KB), ("ng0", KB), ("ng1", KB), ("mixg", KB), ("ffng", KB), ("gateb", 24),
             ("confw", CB * CONF_TAPS), ("confb", CB), ("lng", CB), ("lnb", CB), ("scw", CB * SC_TAPS),
             ("qg", 1), ("kg", 1), ("pek", 16), ("pev", 16), ("w2k", 256), ("w2v", 128)]
    out, at = {}, 0
    for name, n in sizes:
        out[name] = (at, n)
        at += n
    return out, at


def const_table():
    sizes = [("ident", P), ("ropec", NT * HD), ("ropes", NT * HD), ("maskc", TRI), ("maskw", TRI),
             ("cmpadd", NT * NC), ("cmp01", NT * NC), ("cmpfix", NT), ("tri", P), ("negone", P), ("stick01", TRI),
             ("stickadd", TRI)]
    out, at = {}, 0
    for name, n in sizes:
        out[name] = (at, n)
        at += n
    return out, at


class Psum:

    KINDS = {"proj": (0, 1), "turn": (2, 3), "score": (4, 5), "out": (6, 7)}

    def __init__(self, tiles, filled, drained):
        self.tiles, self.filled, self.drained = tiles, filled, drained
        self.uses, self.n, self.turns = {}, [0] * 8, dict.fromkeys(self.KINDS, 0)

    def open(self, pe, kind, name):
        banks = self.KINDS[kind]
        b = banks[self.turns[kind] % len(banks)]
        self.turns[kind] += 1
        if self.n[b]:
            pe.wait_ge(self.drained[b], self.n[b])
        self.n[b] += 1
        assert name not in self.uses, name
        self.uses[name] = (b, self.n[b])
        return self.tiles[b]

    def fill(self, ins, name):
        ins.then_inc(self.filled[self.uses[name][0]], 1)

    def wait_filled(self, eng, name):
        b, n = self.uses[name]
        eng.wait_ge(self.filled[b], n)
        return self.tiles[b]

    def drain(self, ins, name):
        ins.then_inc(self.drained[self.uses[name][0]], 1)

    def wait_drained(self, eng, name):
        b, n = self.uses[name]
        eng.wait_ge(self.drained[b], n)


class Order:

    def __init__(self, eng, own):
        self.eng, self.own, self.n, self.last = eng, own, {}, None

    def __call__(self, ins, sem=None):
        sem = self.own if sem is None else sem
        ins.then_inc(sem, 1)
        self.n[id(sem)] = self.n.get(id(sem), 0) + 1
        self.last = (sem, self.n[id(sem)])
        return self.last

    def after(self, token=None):
        token = token or self.last
        if token:
            self.eng.wait_ge(*token)


def two_blocks_kernel(nc, weights, x_in, consts_in, cols_in, bada_in, finalg_in, sinks_in, out):
    chunks = chunk_table()
    index = {c[0]: n for n, c in enumerate(chunks)}
    cols, n_cols = column_table()
    cst, n_cst = const_table()

    with ExitStack() as ctx:
        def sb(name, shape, dt=F32):
            return ctx.enter_context(nc.sbuf_tensor(name, shape, dt))

        def sem(name):
            return ctx.enter_context(nc.semaphore(name))

        ring = sb("ring", [P, RING, CHUNK])
        X = sb("X", [P, NT, D])
        XH = sb("XH", [P, NT, D])
        HT = sb("HT", [P, KB, S])
        CST, COL = sb("CST", [P, n_cst]), sb("COL", [P, n_cols])
        ONES = sb("ONES", [P, P])
        HALFNEG = sb("HALFNEG", [P, 8])
        GATE, FING = sb("GATE", [P, D]), sb("FING", [P, D])
        SINK, NSINK = sb("SINK", [P, A_HEADS]), sb("NSINK", [P, A_HEADS])
        CACT, CTMP = sb("CACT", [P, KB]), sb("CTMP", [P, KB])
        ADA, MOD = sb("ADA", [P, 2 * KB]), sb("MOD", [P, KB])
        SQ, MS, RS = sb("SQ", [P, 16]), sb("MS", [P, 16, 8]), sb("RS", [P, 16, 8])
        ROT1, ROT2 = sb("ROT1", [P, 512]), sb("ROT2", [P, 512])
        QR = sb("QR", [P, 2, 512])
        G3 = sb("G3", [P, NT, 24])
        QT, KT, OT = sb("QT", [P, KB, S]), sb("KT", [P, KB, S]), sb("OT", [P, KB, S])
        V = sb("V", [P, NT, D])
        ZS = sb("ZS", [P, KB, S])
        ZT = sb("ZT", [P, 2, 512])
        E, PR, PT = sb("E", [P, 3, TRI]), sb("PR", [P, 3, TRI]), sb("PT", [P, 2, TRI])
        n_units = A_HEADS + 2 * B_HEADS + C_HEADS
        NM, DEN, ES = sb("NM", [P, n_units, 2]), sb("DEN", [P, n_units, 2]), sb("ES", [P, A_HEADS, 2])
        BIG = sb("BIG", [P, 24 * S])
        taken = [0]

        def part(*shape, of=None):
            n = int(np.prod(shape))
            a = taken[0]
            taken[0] += n
            assert taken[0] <= 24 * S
            names = "abcd"[:len(shape)]
            if len(shape) == 1:
                return BIG[:, a:a + n]
            return BIG[:, a:a + n].rearrange(f"p ({' '.join(names)}) -> p {' '.join(names)}",
                                             **dict(zip(names, shape)))

        ACC = part(3 * D)
        KR = part(NT, 7, 2 * HD)
        VCD = sb("VCD", [P, NT, 2, 2, HD])
        UP = sb("UP", [P, 4, P])
        U = sb("U", [P, 4, 16, NC])
        HX, HQ, HTH = sb("HX", [P, 4 * NC]), sb("HQ", [P, 4 * NC]), sb("HTH", [P, 4 * NC])
        HID, HID4 = sb("HID", [P, 2, 4 * NC]), sb("HID4", [P, 2, 2, 4, 32])
        KCT, VCM = sb("KCT", [P, 2, NC]), sb("VCM", [P, 2, HD])
        CE, CP = sb("CE", [P, NT, B_HEADS, NC]), sb("CP", [P, NT, B_HEADS, 32])
        CM, CPT = sb("CM", [P, 4, NT, B_HEADS]), sb("CPT", [P, 2, S])
        HB, SB = sb("HB", [P, CB, CONF_TAPS - 1 + S]), sb("SB", [P, CB, SC_TAPS - 1 + S])
        CV, SV = QT[:, CB:2 * CB, :], KT[:, CB:2 * CB, :]
        VALH = ZS
        LNH, LNY = V[:, :, 512:1024], ZS[:, CB:2 * CB, :]
        STAT = sb("STAT", [P, NT, 8])
        GBH, LGH, LBH, QKG = sb("GBH", [P, 24]), sb("LGH", [P, CB]), sb("LBH", [P, CB]), sb("QKG", [P, 2])
        MT = HT
        SCX = OT[:, CB:2 * CB, :]
        GT = BIG[:, :].rearrange("p (k s) -> p k s", k=24)
        tiles = [ctx.enter_context(nc.psum_tensor(f"bank{i}", [P, 512], F32)) for i in range(8)]
        ps = Psum(tiles, [sem(f"filled{i}") for i in range(8)], [sem(f"drained{i}") for i in range(8)])

        params_in, sinks_got, bias_in, fing_in, x_got = (sem("params_in"), sem("sinks_got"), sem("bias_in"),
                                                         sem("fing_in"), sem("x_got"))
        chunk_in = [sem(f"chunk_in{r}") for r in range(RING)]
        dve_step, act_step = sem("dve_step"), sem("act_step")
        consts_set, acc_clear, ada_summed = sem("consts_set"), sem("acc_clear"), sem("ada_summed")
        cact_half, cact_tanh, mod_ready = sem("cact_half"), sem("cact_tanh"), sem("mod_ready")
        squares, means, rstds, x_hat, x_new = sem("squares"), sem("means"), sem("rstds"), sem("x_hat"), sem("x_new")
        v_copied, gate_tanh, roped = sem("v_copied"), sem("gate_tanh"), sem("roped")
        u_built, hid_in, hid_tanh, hid_done = sem("u_built"), sem("hid_in"), sem("hid_tanh"), sem("hid_done")
        cmp_masked, cmp_exp, cmp_probs = sem("cmp_masked"), sem("cmp_exp"), sem("cmp_probs")
        masked, exp_done, probs, pv_done = sem("masked"), sem("exp_done"), sem("probs"), sem("pv_done")
        attn_out, tanh_done, gated = sem("attn_out"), sem("tanh_done"), sem("gated")
        qk_sq, qk_hat, half_cols = sem("qk_sq"), sem("qk_hat"), sem("half_cols")
        conv_done, ln_hat, ln_tanh, ln_done, sc_done = (sem("conv_done"), sem("ln_hat"), sem("ln_tanh"),
                                                        sem("ln_done"), sem("sc_done"))
        soft_ln, soft_masked, rest_sum, stick_p = sem("soft_ln"), sem("soft_masked"), sem("rest_sum"), sem("stick_p")
        merged, ff_read, stored = sem("merged"), sem("ff_read"), sem("stored")

        def const(name, rows=slice(None)):
            a, n = cst[name]
            return CST[rows, a:a + n]

        def col(name):
            a, n = cols[name]
            return COL[:, a:a + n]

        def chunk(name):
            n = index[name]
            _, kb, w = chunks[n]
            return ring[:, n % RING, 0:kb * w].rearrange("p (k c) -> p k c", k=kb)

        def wait_chunk(eng, name):
            n = index[name]
            eng.wait_ge(chunk_in[n % RING], 16 * (n // RING + 1))

        readers = {}

        ident = const("ident")

        def unit(q, k, v, mask, o, first, last, sink=None, gate=None):
            return dict(q=q, k=k, v=v, mask=mask, o=o, first=first, last=last, sink=sink, gate=gate)

        even, odd = [], []
        for h in range(A_HEADS):
            even.append(unit(h, 2, 2, "maskw", h // 2, True, True, sink=h))
        for h in range(B_HEADS):
            g = h // (B_HEADS // B_GROUPS)
            even.append(unit(A_HEADS + h, g, g, "maskc", 4 + h // 2, False, False, gate=3 * h + 1))
            even.append(unit(A_HEADS + h, 3 + g, 3 + g, "maskc", 4 + h // 2, False, True, gate=3 * h + 2))
        for h in range(C_HEADS):
            odd.append(unit(h, None, h, "maskc", h // 2, True, True))
        units = even + odd
        powers = [f"{n}_{t}" for n in ("n0", "n1", "nf", "n2", "q", "k", "ln", "n3") for t in range(NT)]
        rot_order = [("kcks", 0), ("kcks", 1), ("kakw", 0), ("kakw", 1), ("qa", 0), ("qa", 1), ("qb", 0), ("qb", 1)]
        rot_order += [(f"{n}1_{g}", t) for g in range(2) for n in "qk" for t in range(NT)]
        rot_index = {r: n for n, r in enumerate(rot_order)}

        spans = ((0, len(even)), (len(even), len(units)))
        pv_at, stick_pv_at, pv_count = {}, {}, [0]

        block = ctx.enter_context(nc.Block())

        @block.tensor
        def _(pe):
            def by_tokens(name, t, width=512):
                w = chunk(name)
                wait_chunk(pe, name)
                bank = ps.open(pe, "proj", f"{name}.{t}")
                for k in range(KB):
                    mm = pe.matmul(bank[:, 0:width], lhsT=HT[:, k, t * P:(t + 1) * P], rhs=w[:, k, 0:width],
                                   start=(k == 0), stop=(k == KB - 1))
                ps.fill(mm, f"{name}.{t}")
                readers[name] = f"{name}.{t}"

            def by_features(name, j, src=HT, use=None, kb=KB):
                w = chunk(name)
                wait_chunk(pe, name)
                use = use or f"{name}.{j}"
                bank = ps.open(pe, "proj", use)
                for b in range(2):
                    f = (2 * j + b) * P
                    for k in range(kb):
                        mm = pe.matmul(bank[:, b * S:(b + 1) * S], lhsT=w[:, k, f:f + P], rhs=src[:, k, :],
                                       start=(k == 0), stop=(k == kb - 1))
                ps.fill(mm, use)
                readers[name] = use

            def turn(use, blocks, waits=()):
                bank = ps.open(pe, "turn", use)
                for sem_, n in waits:
                    pe.wait_ge(sem_, n)
                for j, src in enumerate(blocks):
                    mm = pe.transpose(bank[:, j * P:(j + 1) * P], src, ident)
                ps.fill(mm, use)

            def norm(n, hat):
                for t in range(NT):
                    for half in range(2):
                        turn(f"n{n}.{t}.{half}", [XH[:, t, (4 * half + j) * P:(4 * half + j + 1) * P] for j in range(4)],
                             [(x_hat, hat + t + 1)])

            def normed(n):
                for t in range(NT):
                    for half in range(2):
                        ps.wait_drained(pe, f"n{n}.{t}.{half}")

            def conditioning(layer):
                pe.wait_ge(ada_summed, 6 * layer + 4)
                bank = ps.open(pe, "proj", f"ada{layer}")
                for j in range(2 * KB):
                    mm = pe.matmul(bank[:, j:j + 1], lhsT=ACC[:, j * P:(j + 1) * P], rhs=ONES[:, 0:1],
                                   start=True, stop=True)
                ps.fill(mm, f"ada{layer}")

            def gate_rows(layer):
                pe.wait_ge(ada_summed, 6 * layer + 6)
                for c in range(2):
                    bank = ps.open(pe, "proj", f"gate{layer}.{c}")
                    mm = pe.matmul(bank[:, :], lhsT=ONES[:, :], rhs=ACC[:, (4 + c) * 512:(5 + c) * 512],
                                   start=True, stop=True)
                    ps.fill(mm, f"gate{layer}.{c}")

            def key_turns():
                items = [(h, t) for h in range(2, 7) for t in range(NT)]
                for n in range(0, len(items), 4):
                    turn(f"kt.{n // 4}", [KR[:, t, h, :] for h, t in items[n:n + 4]], [(roped, 4)])

            def pair_turn(t):
                pe.wait_ge(v_copied, t + 1)
                turn(f"up.{t}", [KR[:, t, 0, :], KR[:, t, 1, :], VCD[:, t, 0, :, :].rearrange("p a d -> p (a d)"),
                                 VCD[:, t, 1, :, :].rearrange("p a d -> p (a d)")], [(roped, t + 1)])

            def head_turn(name, t):
                i = rot_index[(name, t)]
                turn(f"{name}.{t}.T", [QR[:, i % 2, j * P:(j + 1) * P] for j in range(4)], [(roped, i + 1)])

            def half_of(h, tile, blk, a, b):
                r = slice(HD * (h % 2), HD * (h % 2) + HD)
                return tile[r, blk, a:b]

            def scores(u):
                x = units[u]
                q, k = x["q"], x["k"]
                kb = q // 2 if k is None else k
                bank = ps.open(pe, "score", f"s.{u}")
                pe.matmul(bank[:, 0:P], lhsT=half_of(q, QT, q // 2, 0, P), rhs=half_of(q, KT, kb, 0, P),
                          start=True, stop=True)
                mm = pe.matmul(bank[:, P:TRI], lhsT=half_of(q, QT, q // 2, P, S), rhs=half_of(q, KT, kb, 0, S),
                               start=True, stop=True)
                ps.fill(mm, f"s.{u}")

            def probs_turn(u):
                p = PR[:, u % 3, :]
                turn(f"pt.{u}", [p[:, j * P:(j + 1) * P] for j in (0, 1, 2)], [(probs, 2 * u + 2)])

            def weigh(u, base):
                x = units[u]
                q, v, layer = x["q"], x["v"], base
                use = f"o{layer}.{x['o']}"
                r = slice(HD * (q % 2), HD * (q % 2) + HD)
                if x["first"] and q % 2 == 0 or (x["gate"] is not None and not x["last"] and q % 2 == 0):
                    ps.open(pe, "out", use)
                bank = tiles[ps.uses[use][0]]
                started = False
                if x["gate"] is not None and not x["last"]:
                    h = q - A_HEADS
                    ps.wait_drained(pe, "cmpT")
                    rows = slice(32 * (h % 4), 32 * (h % 4) + 32)
                    pe.matmul(bank[r, 0:S], lhsT=VCM[rows, h // 4, :], rhs=CPT[rows, h // 4, :],
                              start=True, stop=False)
                    started = True
                ps.wait_drained(pe, f"pt.{u}")
                pt = PT[:, u % 2, :]
                pe.matmul(bank[r, 0:S], lhsT=V[:, 0, v * HD:(v + 1) * HD], rhs=pt[:, 0:S],
                          start=(x["first"] and not started), stop=False)
                mm = pe.matmul(bank[r, P:S], lhsT=V[:, 1, v * HD:(v + 1) * HD], rhs=pt[:, S:TRI],
                               start=False, stop=x["last"])
                if x["last"] and q % 2 == 1:
                    ps.fill(mm, use)
                    pv_at[u] = None
                else:
                    mm.then_inc(pv_done, 1)
                    pv_at[u] = pv_count[0] = pv_count[0] + 1

            def second_half():
                for use in ("q1_1.0.T", "q1_1.1.T", "k1_1.0.T", "k1_1.1.T", "v1_1.0", "v1_1.1"):
                    ps.wait_drained(pe, use)

            def attention(layer, extra):
                a, b = spans[layer]
                for i in range(a, b + 3):
                    if layer == 1 and i - a == KB:
                        second_half()
                    if i < b:
                        scores(i)
                    for what in extra.get(i - a, ()):
                        what()
                    if a <= i - 2 < b:
                        probs_turn(i - 2)
                    if a <= i - 3 < b:
                        weigh(i - 3, layer)

            def output(layer, src):
                for t in range(NT):
                    for c in range(2):
                        name = f"wo{layer}_{c}" if layer < 2 else f"wf{c}"
                        w = chunk(name)
                        wait_chunk(pe, name)
                        use = f"y{layer}.{t}.{c}"
                        bank = ps.open(pe, "proj", use)
                        for k in range(KB):
                            mm = pe.matmul(bank[:, :], lhsT=src[:, k, t * P:(t + 1) * P], rhs=w[:, k, :],
                                           start=(k == 0), stop=(k == KB - 1))
                        ps.fill(mm, use)
                        readers[name] = use

            def compress_in(kv):
                name = ("w1k", "w1v")[kv]
                w = chunk(name)
                wait_chunk(pe, name)
                pe.wait_ge(u_built, 2 * kv + 2)
                bank = ps.open(pe, "proj", f"hid.{kv}")
                for hb in range(2):
                    for j in range(16):
                        mm = pe.matmul(bank[:, hb * 2 * NC:(hb + 1) * 2 * NC], lhsT=w[:, j, hb * P:(hb + 1) * P],
                                       rhs=U[:, 2 * kv:2 * kv + 2, j, :], start=(j == 0), stop=(j == 15))
                ps.fill(mm, f"hid.{kv}")
                readers[name] = f"hid.{kv}"

            def compress_out():
                pe.wait_ge(hid_done, 1)
                bank = ps.open(pe, "proj", "kc2")
                for hb in range(2):
                    mm = pe.matmul(bank[:, 0:2 * NC], lhsT=col("w2k")[:, hb * P:(hb + 1) * P],
                                   rhs=HID[:, 0, hb * 2 * NC:(hb + 1) * 2 * NC], start=(hb == 0), stop=(hb == 1))
                ps.fill(mm, "kc2")
                pe.wait_ge(hid_done, 3)
                bank = ps.open(pe, "proj", "vc2")
                for g in range(2):
                    for hb in range(2):
                        mm = pe.matmul(bank[:, g * HD:(g + 1) * HD],
                                       lhsT=HID4[:, hb, g, :, :].rearrange("p a c -> p (a c)"),
                                       rhs=col("w2v")[:, hb * HD:(hb + 1) * HD], start=(hb == 0), stop=(hb == 1))
                ps.fill(mm, "vc2")

            def compressed_scores():
                ps.wait_drained(pe, "kc2")
                ps.wait_drained(pe, "qb.0.T")
                ps.wait_drained(pe, "qb.1.T")
                for half in range(2):
                    bank = ps.open(pe, "proj", f"cmp.{half}")
                    r = slice(HD * half, HD * half + HD)
                    for t in range(NT):
                        for j in range(B_HEADS // 2):
                            a = (t * (B_HEADS // 2) + j) * NC
                            mm = pe.matmul(bank[:, a:a + NC], lhsT=QT[r, 4 + j, t * P:(t + 1) * P],
                                           rhs=KCT[r, j // 2, :], start=True, stop=True)
                    ps.fill(mm, f"cmp.{half}")

            def compressed_turn():
                ps.wait_drained(pe, "vc2")
                turn("cmpT", [CP[:, t, 4 * g:4 * g + 4, :].rearrange("p h c -> p (h c)")
                              for g in range(2) for t in range(NT)], [(cmp_probs, 1)])

            pe.wait_ge(params_in, 32)
            pe.wait_ge(consts_set, 4)

            conditioning(0)
            norm(0, 0)
            normed(0)
            turns = {1: lambda: pair_turn(0), 2: lambda: pair_turn(1), 4: key_turns, 5: lambda: head_turn("qa", 0),
                     6: lambda: head_turn("qa", 1), 7: lambda: head_turn("qb", 0)}
            for n, (name, t) in enumerate(rot_order[:8]):
                by_tokens(name, t, 408 if name == "kakw" else 512)
                if n in turns:
                    turns[n]()
                if n == 5:
                    gate_rows(0)
            compress_in(0)
            head_turn("qb", 1)
            compress_in(1)
            for n in range(3):
                ps.wait_drained(pe, f"kt.{n}")
            for t in range(NT):
                ps.wait_drained(pe, f"qa.{t}.T")
            attention(0, {0: [lambda: by_features("za", 0)], 1: [lambda: by_features("za", 1)], 3: [compress_out],
                          5: [compressed_scores], 8: [compressed_turn, lambda: by_features("zb", 0)],
                          10: [lambda: by_features("zb", 1)]})
            for o in range(KB):
                ps.wait_drained(pe, f"o0.{o}")
            output(0, OT)

            conditioning(1)
            norm(1, 2)
            gate_rows(1)
            normed(1)
            by_tokens("q1_0", 0)
            by_tokens("q1_0", 1)
            by_tokens("k1_0", 0)
            head_turn("q1_0", 0)
            by_tokens("k1_0", 1)
            head_turn("q1_0", 1)
            by_tokens("v1_0", 0)
            head_turn("k1_0", 0)
            by_tokens("v1_0", 1)
            head_turn("k1_0", 1)
            for use in ("q1_0.0.T", "q1_0.1.T", "k1_0.0.T", "k1_0.1.T", "v1_0.0", "v1_0.1"):
                ps.wait_drained(pe, use)

            attention(1, {0: [lambda: by_features("z1_0", 0)], 1: [lambda: by_features("z1_0", 1)],
                          2: [lambda: by_tokens("q1_1", 0)], 3: [lambda: by_tokens("q1_1", 1)],
                          4: [lambda: by_tokens("k1_1", 0), lambda: head_turn("q1_1", 0)],
                          5: [lambda: by_tokens("k1_1", 1), lambda: head_turn("q1_1", 1)],
                          6: [lambda: by_tokens("v1_1", 0), lambda: head_turn("k1_1", 0)],
                          7: [lambda: by_tokens("v1_1", 1), lambda: head_turn("k1_1", 1)],
                          9: [lambda: by_features("z1_1", 0)], 11: [lambda: by_features("z1_1", 1)]})
            for o in range(KB):
                ps.wait_drained(pe, f"o1.{o}")
            output(1, OT)

            norm(2, 4)
            normed(2)
            for name in ("val", "cga"):
                by_features(name, 0)
                by_features(name, 1)

            def qk_turn(name, t):
                i = 2 * (name == "k2") + t
                turn(f"{name}.{t}.T", [QR[:, i % 2, j * P:(j + 1) * P] for j in range(4)], [])

            by_tokens("q2", 0)
            by_tokens("q2", 1)
            ps.wait_drained(pe, "q2.0")
            qk_turn("q2", 0)
            by_tokens("k2", 0)
            ps.wait_drained(pe, "q2.1")
            qk_turn("q2", 1)
            by_tokens("k2", 1)
            ps.wait_drained(pe, "k2.0")
            qk_turn("k2", 0)
            by_tokens("v2", 0)
            ps.wait_drained(pe, "k2.1")
            qk_turn("k2", 1)
            by_tokens("v2", 1)
            for name in ("scx", "scg", "sbg"):
                by_features(name, 0)
                by_features(name, 1)
            for g in range(6):
                by_features(f"g{g}", 0)
                by_features(f"g{g}", 1)
            pe.wait_ge(conv_done, 1)
            for t in range(NT):
                turn(f"ln.{t}", [CV[:, b, t * P:(t + 1) * P] for b in range(CB)])
            for t in range(NT):
                ps.wait_drained(pe, f"ln.{t}")
                turn(f"lnT.{t}", [LNH[:, t, b * P:(b + 1) * P] for b in range(CB)])

            def stick_scores(h):
                bank = ps.open(pe, "score", f"z.{h}")
                pe.matmul(bank[:, 0:S], lhsT=half_of(h, KT, h // 2, 0, P), rhs=half_of(h, QT, h // 2, 0, S),
                          start=True, stop=True)
                mm = pe.matmul(bank[:, S:TRI], lhsT=half_of(h, KT, h // 2, P, S), rhs=half_of(h, QT, h // 2, P, S),
                               start=True, stop=True)
                ps.fill(mm, f"z.{h}")

            def stick_rest(h):
                bank = ps.open(pe, "turn", f"r.{h}")
                pe.wait_ge(soft_masked, h + 1)
                l = E[:, h % 3, :]
                pe.matmul(bank[:, 0:S], lhsT=const("tri"), rhs=l[:, 0:S], start=True, stop=False)
                pe.matmul(bank[:, P:S], lhsT=const("negone"), rhs=l[:, S:TRI], start=False, stop=True)
                mm = pe.matmul(bank[:, S:TRI], lhsT=const("tri"), rhs=l[:, S:TRI], start=True, stop=True,
                               skip_group_check=True)
                ps.fill(mm, f"r.{h}")

            def stick_weigh(h):
                use = f"so.{h // 2}"
                if h % 2 == 0:
                    ps.open(pe, "out", use)
                bank = tiles[ps.uses[use][0]]
                r = slice(HD * (h % 2), HD * (h % 2) + HD)
                pe.wait_ge(stick_p, h + 1)
                pt = PT[:, h % 2, :]
                pe.matmul(bank[r, 0:S], lhsT=V[:, 0, h * HD:(h + 1) * HD], rhs=pt[:, 0:S], start=True, stop=False)
                mm = pe.matmul(bank[r, P:S], lhsT=V[:, 1, h * HD:(h + 1) * HD], rhs=pt[:, S:TRI],
                               start=False, stop=True)
                if h % 2:
                    ps.fill(mm, use)
                else:
                    mm.then_inc(pv_done, 1)
                    pv_count[0] += 1
                    stick_pv_at[h] = pv_count[0]

            def branch(name, j, src):
                if name == "cfo" and j == 0:
                    pe.wait_ge(ln_done, NT)
                by_features(name, j, src, kb=4)

            for name, n in (("q2.0.T", 0), ("q2.1.T", 0), ("k2.0.T", 0), ("k2.1.T", 0), ("v2.0", 0), ("v2.1", 0)):
                ps.wait_drained(pe, name)
            for j in range(2):
                ps.wait_drained(pe, f"sbg.{j}")
            for i in range(S_HEADS + 4):
                if i < S_HEADS:
                    stick_scores(i)
                if i < 4:
                    branch("sco", i, SV)
                elif i < 8:
                    branch("cfo", i - 4, LNY)
                if 0 <= i - 2 < S_HEADS:
                    stick_rest(i - 2)
                if 0 <= i - 4 < S_HEADS:
                    stick_weigh(i - 4)
            for o in range(4):
                ps.wait_drained(pe, f"so.{o}")
            for j in range(4):
                branch("ato", j, OT)
            pe.wait_ge(merged, 4)
            output(2, MT)
            norm(3, 6)
            normed(3)
            for i in range(FB // 2):
                by_features(f"fi{i}", 0, use=f"fg.{i}")
                by_features(f"fi{i}", 1, use=f"fu.{i}")
            banks = [ps.open(pe, kind, f"ff.{n}") for n, kind in enumerate(("score", "score", "out", "out"))]
            AT = BIG[:, :].rearrange("p (k s) -> p k s", k=24)
            for i in range((FB + 3) // 4):
                name = f"fo{i}"
                wait_chunk(pe, name)
                w = chunk(name)
                n = min(4, FB - 4 * i)
                for k in range(n):
                    ps.wait_drained(pe, f"fu.{(4 * i + k) // 2}")
                order = [(k, t, c) for k in range(n) for t in range(NT) for c in range(2)]
                if 4 * i + n == FB:
                    order = [(k, t, c) for t in range(NT) for c in range(2) for k in range(n)]
                for k, t, c in order:
                    kk = 4 * i + k
                    mm = pe.matmul(banks[2 * t + c][:, :], lhsT=AT[:, kk, t * P:(t + 1) * P],
                                   rhs=w[:, k, c * 512:(c + 1) * 512], start=(kk == 0), stop=(kk == FB - 1))
                    if kk == FB - 1:
                        ps.fill(mm, f"ff.{2 * t + c}")
                    elif (k, t, c) == order[-1]:
                        mm.then_inc(ff_read, 1)
                readers[name] = ("ff_read", i + 1)

        @block.sync
        def _(sp):
            for n, (name, kb, width) in enumerate(chunks):
                if n >= RING:
                    old = chunks[n - RING][0]
                    if old.startswith("ada"):
                        layer, c = int(old[3]), int(old[5])
                        sp.wait_ge(ada_summed, 6 * layer + c + 1)
                    elif isinstance(readers[old], tuple):
                        sp.wait_ge(ff_read, readers[old][1])
                    else:
                        ps.wait_filled(sp, readers[old])
                sp.dma_start(ring[:, n % RING, 0:kb * width], weights[n, :, 0:kb * width]).then_inc(chunk_in[n % RING], 16)
            for t in range(NT):
                for c in range(2):
                    ps.wait_drained(sp, f"ff.{2 * t + c}")
                sp.dma_start(out[0, t * P:(t + 1) * P, :], X[:, t, :]).then_inc(stored, 16)
            sp.wait_ge(stored, 16 * NT)

        @block.gpsimd
        def _(pool):
            pool.memset(ACC[:, :], 0.0).then_inc(acc_clear, 1)
            pool.dma_start(X[:, :, :], x_in[0].rearrange("(t p) d -> p t d", t=NT)).then_inc(x_got, 16)
            pool.dma_start(COL[:, :], cols_in).then_inc(params_in, 16)
            pool.dma_start(CST[:, :], consts_in).then_inc(params_in, 16)
            pool.wait_ge(acc_clear, 1)
            pool.dma_start(ACC[0:1, :], bada_in[0:1, :]).then_inc(bias_in, 16)
            pool.dma_start(SINK[:, :], sinks_in.partition_broadcast(P)).then_inc(sinks_got, 16)
            pool.dma_start(FING[:, :], finalg_in.partition_broadcast(P)).then_inc(fing_in, 16)
            pool.memset(ONES[:, :], 1.0).then_inc(consts_set, 1)
            pool.memset(HALFNEG[:, :], -0.5).then_inc(consts_set, 1)
            pool.memset(CP[:, :, :, :], 0.0).then_inc(consts_set, 1)
            pool.memset(HID4[:, :, :, :, :], 0.0).then_inc(consts_set, 1)
            pool.memset(HB[:, :, 0:CONF_TAPS - 1], 0.0).then_inc(consts_set, 1)
            pool.memset(SB[:, :, 0:SC_TAPS - 1], 0.0).then_inc(consts_set, 1)
            pool.wait_ge(consts_set, 2)
            for n, name in enumerate(powers):
                if name == "n1_0":
                    ps.wait_filled(pool, "gate0.0")
                    ps.wait_filled(pool, "gate0.1")
                    pool.memset(ACC[:, :], 0.0).then_inc(acc_clear, 1)
                    pool.wait_ge(acc_clear, 2)
                    pool.dma_start(ACC[0:1, :], bada_in[1:2, :]).then_inc(bias_in, 16)
                w = S_HEADS if name[0] in "qk" else 1
                pool.wait_ge(means, n + 1)
                pool.tensor_tensor(RS[:, n, 0:w], MS[:, n, 0:w], HALFNEG[:, 0:w], ALU.pow).then_inc(rstds, 1)

        @block.scalar
        def _(act):
            do = Order(act, act_step)
            n_sq = [0]

            def square(name, t):
                do.after()
                do(act.activation(ZS[:, 4 * t:4 * t + 4, :], X[:, t, :].rearrange("p (k s) -> p k s", k=4), ACT.Square,
                                  accum_out=SQ[:, powers.index(f"{name}_{t}"):powers.index(f"{name}_{t}") + 1]), squares)

            def evict_norm(n):
                for t in range(NT):
                    bank = ps.wait_filled(act, f"n{n}.{t}.1")
                    for j in range(4):
                        b = 4 + j
                        scale = MOD[:, b:b + 1] if n < 2 else col("mixg" if n == 2 else "ffng")[:, b:b + 1]
                        shift = ADA[:, b:b + 1] if n < 2 else 0.0
                        ins = act.activation(HT[:, b, t * P:(t + 1) * P], bank[:, j * P:(j + 1) * P], ACT.Identity,
                                             scale=scale, bias=shift)
                        if j < 3:
                            do(ins)
                        else:
                            ps.drain(ins, f"n{n}.{t}.1")

            def evict(use, dst, src=None, scale=1.0):
                bank = ps.wait_filled(act, use)
                src = bank[:, :] if src is None else src(bank)
                ps.drain(act.activation(dst, src, ACT.Copy, scale=scale), use)

            def flat4(bank):
                return bank[:, :].rearrange("p (b s) -> p b s", b=4)

            def flat2(bank):
                return bank[:, :].rearrange("p (b s) -> p b s", b=2)

            def head_turn(name, t):
                i = rot_index[(name, t)]
                dst = KT if name[0] == "k" else QT
                base = 4 if name == "qb" or name.endswith("_1") else 0
                evict(f"{name}.{t}.T", dst[:, base:base + 4, t * P:(t + 1) * P], flat4)

            def gate_half(use, j):
                evict(use, ZS[:, 2 * j:2 * j + 2, :], flat2, scale=0.5)
                if gates_made[0] >= 2:
                    act.wait_ge(gated, gates_made[0] - 1)
                ps.wait_drained(act, use)
                do(act.activation(ZT[:, gates_made[0] % 2, :].rearrange("p (b s) -> p b s", b=2), ZS[:, 2 * j:2 * j + 2, :],
                                  ACT.Tanh), tanh_done)
                gates_made[0] += 1

            gates_made = [0]

            def exps(u):
                x = units[u]
                if u >= 3:
                    ps.wait_filled(act, f"pt.{u - 3}")
                ps.wait_drained(act, f"s.{u}")
                if x["sink"] is not None:
                    h = x["sink"]
                    act.wait_ge(masked, h + 1)
                    do(act.activation(ES[:, h, :], NM[:, u, :], ACT.Exp, bias=SINK[:, h:h + 1]))
                do(act.activation(PR[:, u % 3, 0:P], E[:, u % 3, 0:P], ACT.Exp, scale=-1.0, bias=NM[:, u, 0:1],
                                  accum_out=DEN[:, u, 0:1]))
                do(act.activation(PR[:, u % 3, P:TRI], E[:, u % 3, P:TRI], ACT.Exp, scale=-1.0, bias=NM[:, u, 1:2],
                                  accum_out=DEN[:, u, 1:2]), exp_done)

            def probs_copy(u):
                ps.wait_filled(act, f"pt.{u}")
                if u >= 2:
                    if pv_at[u - 2] is None:
                        x = units[u - 2]
                        ps.wait_filled(act, f"o{0 if u - 2 < spans[0][1] else 1}.{x['o']}")
                    else:
                        act.wait_ge(pv_done, pv_at[u - 2])
                evict(f"pt.{u}", PT[:, u % 2, :], lambda bank: bank[:, 0:TRI])

            def attention(layer, extra):
                a, b = spans[layer]
                for i in range(a, b + 3):
                    if i < b:
                        exps(i)
                    if a <= i - 2 < b:
                        probs_copy(i - 2)
                    for what in extra.get(i - a, ()):
                        what()

            act.wait_ge(cact_half, 1)
            do(act.activation(CACT[:, :], CTMP[:, :], ACT.Tanh), cact_tanh)
            act.wait_ge(x_got, 16)
            for t in range(NT):
                square("n0", t)
            act.wait_ge(mod_ready, 1)
            evict_norm(0)

            def values_out(t):
                bank = ps.wait_filled(act, f"kcks.{t}")
                do(act.activation(VCD[:, t, :, :, :], bank[:, 256:384].rearrange("p (g d) -> p g d", g=2).unsqueeze(2)
                                  .to_broadcast([P, 2, 2, HD]), ACT.Copy))
                do(act.activation(V[:, t, 0:P], bank[:, 384:512], ACT.Copy), v_copied)

            def values_out2(t):
                bank = ps.wait_filled(act, f"kakw.{t}")
                do(act.activation(V[:, t, P:P + 192], bank[:, 192:384], ACT.Copy))
                do(act.activation(G3[:, t, :], bank[:, 384:408], ACT.Tanh, scale=0.5), v_copied)

            def pair_out(t):
                bank = ps.wait_filled(act, f"up.{t}")
                v = bank[:, :].rearrange("p (b i l) -> p b i l", b=4, l=2)
                do(act.activation(UP[0:HD, :, t * 64:(t + 1) * 64], v[0:HD, :, :, 0], ACT.Copy))
                ps.drain(act.activation(UP[HD:P, :, t * 64:(t + 1) * 64], v[HD:P, :, :, 1], ACT.Copy), f"up.{t}")

            def keys_out(n):
                w = min(4, 10 - 4 * n)
                evict(f"kt.{n}", KT[:, 0:5, :].rearrange("p h (t s) -> p (h t) s", t=NT)[:, 4 * n:4 * n + w, :],
                      lambda bank: bank[:, 0:w * P].rearrange("p (b s) -> p b s", b=w))

            values_out(0)
            values_out(1)
            pair_out(0)
            values_out2(0)
            pair_out(1)
            values_out2(1)
            for n in range(3):
                keys_out(n)
            head_turn("qa", 0)
            for c in range(2):
                evict(f"gate0.{c}", GATE[:, c * 512:(c + 1) * 512])
            head_turn("qa", 1)
            head_turn("qb", 0)

            def hidden_tanh(kv):
                act.wait_ge(hid_in, kv + 1)
                do(act.activation(HTH[:, :], HQ[:, :], ACT.Tanh, scale=float(np.sqrt(2 / np.pi))), hid_tanh)

            hidden_tanh(0)
            head_turn("qb", 1)
            hidden_tanh(1)

            def compressed_out():
                evict("kc2", KCT[:, :, :], lambda bank: bank[:, 0:2 * NC].rearrange("p (g c) -> p g c", g=2))
                evict("vc2", VCM[:, :, :], lambda bank: bank[:, 0:P].rearrange("p (g d) -> p g d", g=2))

            def compressed_exp():
                act.wait_ge(cmp_masked, 1)
                do(act.activation(CE[:, :, :, :], CE[:, :, :, :], ACT.Exp, scale=SCALE), cmp_exp)

            attention(0, {0: [lambda: gate_half("za.0", 0)], 1: [lambda: gate_half("za.1", 1)], 3: [compressed_out],
                          6: [compressed_exp],
                          8: [lambda: evict("cmpT", CPT[:, :, :], flat2), lambda: gate_half("zb.0", 2)],
                          10: [lambda: gate_half("zb.1", 3)]})

            for t in range(NT):
                act.wait_ge(x_new, 2 * t + 2)
                square("n1", t)
            act.wait_ge(mod_ready, 2)
            evict_norm(1)
            for c in range(2):
                evict(f"gate1.{c}", GATE[:, c * 512:(c + 1) * 512])

            def values(name, t, base):
                evict(f"{name}.{t}", V[:, t, base:base + 512])

            head_turn("q1_0", 0)
            head_turn("q1_0", 1)
            values("v1_0", 0, 0)
            head_turn("k1_0", 0)
            values("v1_0", 1, 0)
            head_turn("k1_0", 1)
            attention(1, {0: [lambda: gate_half("z1_0.0", 0)], 1: [lambda: gate_half("z1_0.1", 1)],
                          4: [lambda: head_turn("q1_1", 0)], 5: [lambda: head_turn("q1_1", 1)],
                          6: [lambda: values("v1_1", 0, 512), lambda: head_turn("k1_1", 0)],
                          7: [lambda: values("v1_1", 1, 512), lambda: head_turn("k1_1", 1)],
                          9: [lambda: gate_half("z1_1.0", 2)], 11: [lambda: gate_half("z1_1.1", 3)]})

            for t in range(NT):
                act.wait_ge(x_new, 4 + 2 * t + 2)
                square("nf", t)
            for t in range(NT):
                act.wait_ge(x_new, 8 + t + 1)
                square("n2", t)
            evict_norm(2)
            for j in range(2):
                evict(f"val.{j}", VALH[:, 2 * j:2 * j + 2, :], flat2, scale=0.5)
            for j in range(2):
                bank = ps.wait_filled(act, f"cga.{j}")
                ps.drain(act.activation(ZT[:, j, :], bank[:, :], ACT.Tanh, scale=0.5), f"cga.{j}")

            def qk_square(name, t):
                i = 2 * (name == "k2") + t
                bank = ps.wait_filled(act, f"{name}.{t}")
                if i >= 2:
                    ps.wait_drained(act, f"{'q2'}.{t}")
                do(act.activation(LNH[:, i % 2, :], bank[:, :], ACT.Square), qk_sq)

            def qk_turn(name, t):
                use = f"{name}.{t}.T"
                bank = ps.wait_filled(act, use)
                dst = QT if name == "q2" else KT
                g = 0 if name == "q2" else 1
                ps.drain(act.activation(dst[:, 0:4, t * P:(t + 1) * P], flat4(bank), ACT.Identity,
                                        scale=QKG[:, g:g + 1]), use)

            act.wait_ge(half_cols, 1)
            qk_square("q2", 0)
            qk_square("q2", 1)
            qk_turn("q2", 0)
            qk_square("k2", 0)
            qk_turn("q2", 1)
            qk_square("k2", 1)
            qk_turn("k2", 0)
            evict("v2.0", V[:, 0, 0:512])
            qk_turn("k2", 1)
            evict("v2.1", V[:, 1, 0:512])
            for j in range(2):
                evict(f"scx.{j}", SCX[:, 2 * j:2 * j + 2, :], flat2)
            for g in range(6):
                for j in range(2):
                    use = f"g{g}.{j}"
                    bank = ps.wait_filled(act, use)
                    for b in range(2):
                        f = 4 * g + 2 * j + b
                        ins = act.activation(GT[:, f, :], bank[:, b * S:(b + 1) * S], ACT.Tanh, scale=0.5,
                                             bias=GBH[:, f:f + 1])
                        if b == 0:
                            do(ins)
                        else:
                            ps.drain(ins, use)
            for t in range(NT):
                use = f"lnT.{t}"
                bank = ps.wait_filled(act, use)
                for b in range(CB):
                    ins = act.activation(LNY[:, b, t * P:(t + 1) * P], bank[:, b * P:(b + 1) * P], ACT.Identity,
                                         scale=LGH[:, b:b + 1], bias=LBH[:, b:b + 1])
                    if b < CB - 1:
                        do(ins)
                    else:
                        ps.drain(ins, use)
                ps.wait_drained(act, use)
                do(act.activation(ZT[:, t, :].rearrange("p (b s) -> p b s", b=CB), LNY[:, :, t * P:(t + 1) * P], ACT.Tanh),
                   ln_tanh)

            def softplus_log(h):
                bank = ps.wait_filled(act, f"z.{h}")
                b = PR[:, h % 3, :]
                if h >= 3:
                    act.wait_ge(stick_p, h - 2)
                do(act.activation(b, bank[:, 0:TRI], ACT.Abs))
                do.after()
                do(act.activation(b, b, ACT.Exp, scale=-1.0))
                do.after()
                do(act.activation(b, b, ACT.Ln, bias=1.0), soft_ln)

            def stick_exp(h):
                ps.wait_drained(act, f"r.{h}")
                if h >= 2:
                    if h % 2:
                        ps.wait_filled(act, f"so.{(h - 2) // 2}")
                    else:
                        act.wait_ge(pv_done, stick_pv_at[h - 2])
                do(act.activation(PT[:, h % 2, :], PR[:, h % 3, :], ACT.Exp), stick_p)

            for i in range(S_HEADS + 2):
                if i < S_HEADS:
                    softplus_log(i)
                if 0 <= i - 2 < S_HEADS:
                    stick_exp(i - 2)
            for t in range(NT):
                for c in range(2):
                    ps.wait_drained(act, f"y2.{t}.{c}")
                square("n3", t)
            evict_norm(3)
            for i in range(FB // 2):
                if i >= 2:
                    ps.wait_drained(act, f"fu.{i - 2}")
                bank = ps.wait_filled(act, f"fg.{i}")
                ps.drain(act.activation(ZT[:, i % 2, :], bank[:, :], ACT.Silu), f"fg.{i}")

        @block.vector
        def _(dve):
            do = Order(dve, dve_step)

            def ada(layer, c):
                name = f"ada{layer}_{c}"
                w = chunk(name)
                wait_chunk(dve, name)
                dve.wait_ge(bias_in, 16 * (layer + 1))
                acc = ACC[:, c * 512:(c + 1) * 512]
                for k in range(KB):
                    do.after()
                    do(dve.scalar_tensor_tensor(acc, w[:, k, :], CACT[:, k:k + 1], acc, ALU.mult, ALU.add),
                       ada_summed if k == KB - 1 else None)

            sq_seen = [0]

            def stat(name, t):
                i = powers.index(f"{name}_{t}")
                sq_seen[0] += 1
                dve.wait_ge(squares, sq_seen[0])
                do(dve.tensor_scalar(MS[:, i, 0:1], SQ[:, i:i + 1], 1.0 / D, EPS, ALU.mult, ALU.add), means)

            def hat(name, t):
                i = powers.index(f"{name}_{t}")
                dve.wait_ge(rstds, i + 1)
                do(dve.tensor_scalar(XH[:, t, :], X[:, t, :], RS[:, i, 0:1], None, ALU.mult), x_hat)

            def modulation(layer):
                bank = ps.wait_filled(dve, f"ada{layer}")
                ps.drain(dve.tensor_copy(ADA[:, :], bank[:, 0:2 * KB]), f"ada{layer}")
                ps.wait_drained(dve, f"ada{layer}")
                do(dve.scalar_tensor_tensor(MOD[:, :], ADA[:, KB:2 * KB], 1.0, col(f"ng{layer}"), ALU.add, ALU.mult),
                   mod_ready)
                do.after()

            def evict_norm(n):
                for t in range(NT):
                    use = f"n{n}.{t}.0"
                    bank = ps.wait_filled(dve, use)
                    for b in range(4):
                        dst, src = HT[:, b, t * P:(t + 1) * P], bank[:, b * P:(b + 1) * P]
                        if n < 2:
                            ins = dve.tensor_scalar(dst, src, MOD[:, b:b + 1], ADA[:, b:b + 1], ALU.mult, ALU.add)
                        else:
                            g = col("mixg" if n == 2 else "ffng")
                            ins = dve.tensor_scalar(dst, src, g[:, b:b + 1], None, ALU.mult)
                        if b < 3:
                            do(ins)
                        else:
                            ps.drain(ins, use)

            def rotate(name, t):
                i = rot_index[(name, t)]
                use = f"{name}.{t}"
                heads = {"kcks": 4, "kakw": 3}.get(name, 8)
                bank = ps.wait_filled(dve, use)
                x = bank[:, 0:heads * HD].rearrange("p (h u d) -> p h u d", u=2, d=HALF)
                x3 = bank[:, 0:heads * HD].rearrange("p (h d) -> p h d", d=HD)
                c = const("ropec")[:, t * HD:(t + 1) * HD].unsqueeze(1).to_broadcast([P, heads, HD])
                s0 = const("ropes")[:, t * HD:t * HD + HALF].unsqueeze(1).to_broadcast([P, heads, HALF])
                s1 = const("ropes")[:, t * HD + HALF:(t + 1) * HD].unsqueeze(1).to_broadcast([P, heads, HALF])
                r1 = ROT1[:, 0:heads * HD].rearrange("p (h d) -> p h d", d=HD)
                r2 = ROT2[:, 0:heads * HD].rearrange("p (h u d) -> p h u d", u=2, d=HALF)
                if heads < 8:
                    dve.wait_ge(v_copied, i + 1)
                do.after()
                do(dve.tensor_tensor(r1, x3, c, ALU.mult))
                do(dve.tensor_tensor(r2[:, :, 0, :], x[:, :, 1, :], s0, ALU.mult))
                ps.drain(dve.tensor_tensor(r2[:, :, 1, :], x[:, :, 0, :], s1, ALU.mult), use)
                ps.wait_drained(dve, use)
                if heads < 8:
                    base = 0 if name == "kcks" else 4
                    a = ROT1[:, 0:heads * HD].rearrange("p (h d) -> p h d", d=HD).unsqueeze(2).to_broadcast([P, heads, 2, HD])
                    b = ROT2[:, 0:heads * HD].rearrange("p (h d) -> p h d", d=HD).unsqueeze(2).to_broadcast([P, heads, 2, HD])
                    dst = KR[:, t, base:base + heads, :].rearrange("p h (u d) -> p h u d", u=2)
                    do(dve.tensor_tensor(dst, a, b, ALU.add), roped)
                else:
                    if rot_order[i - 2][0] not in ("kcks", "kakw"):
                        n2, t2 = rot_order[i - 2]
                        ps.wait_filled(dve, f"{n2}.{t2}.T")
                    do(dve.tensor_tensor(QR[:, i % 2, :], ROT1[:, :], ROT2[:, :], ALU.add), roped)

            def build_u(kv):
                pe_ = col(("pek", "pev")[kv])
                for m in range(2):
                    src = UP[:, 2 * kv:2 * kv + 2, 8 * m:8 * m + 8 * NC].rearrange("p g (c j) -> p g j c", j=8)
                    emb = pe_[:, 8 * m:8 * m + 8].unsqueeze(1).unsqueeze(3).to_broadcast([P, 2, 8, NC])
                    do(dve.tensor_tensor(U[:, 2 * kv:2 * kv + 2, 8 * m:8 * m + 8, :], src, emb, ALU.add), u_built)

            def hidden(kv):
                bank = ps.wait_filled(dve, f"hid.{kv}")
                do.after()
                ps.drain(dve.tensor_copy(HX[:, :], bank[:, 0:4 * NC]), f"hid.{kv}")
                ps.wait_drained(dve, f"hid.{kv}")
                do(dve.tensor_tensor(HQ[:, :], HX[:, :], HX[:, :], ALU.mult))
                do.after()
                do(dve.tensor_scalar(HQ[:, :], HQ[:, :], 0.044715, 1.0, ALU.mult, ALU.add))
                do.after()
                do(dve.tensor_tensor(HQ[:, :], HQ[:, :], HX[:, :], ALU.mult), hid_in)
                do.after()
                do(dve.tensor_scalar(HX[:, :], HX[:, :], 0.5, None, ALU.mult))

            def hidden_out(kv):
                dve.wait_ge(hid_tanh, kv + 1)
                do.after()
                do(dve.scalar_tensor_tensor(HID[:, kv, :], HTH[:, :], 1.0, HX[:, :], ALU.add, ALU.mult),
                   hid_done if kv == 0 else None)
                if kv:
                    do.after()
                    dve.wait_ge(consts_set, 4)
                    for hb in range(2):
                        src = HID[:, 1, hb * 2 * NC:(hb + 1) * 2 * NC].rearrange("p (g c) -> p g c", g=2)
                        do(dve.tensor_copy(HID4[:, hb, :, :, 0:NC], src.unsqueeze(2).to_broadcast([P, 2, 4, NC])), hid_done)

            def mask_scores(u):
                x = units[u]
                bank = ps.wait_filled(dve, f"s.{u}")
                e = E[:, u % 3, :]
                m = const(x["mask"])
                do(dve.tensor_tensor_reduce(e[:, 0:P], bank[:, 0:P], m[:, 0:P], -SCALE, 3e38, ALU.add, ALU.min,
                                            NM[:, u, 0:1]))
                ps.drain(dve.tensor_tensor_reduce(e[:, P:TRI], bank[:, P:TRI], m[:, P:TRI], -SCALE, 3e38, ALU.add,
                                                  ALU.min, NM[:, u, 1:2]), f"s.{u}")
                if x["sink"] is not None:
                    ps.wait_drained(dve, f"s.{u}")
                    h = x["sink"]
                    do(dve.tensor_scalar(NM[:, u, :], NM[:, u, :], NSINK[:, h:h + 1], None, ALU.min), masked)

            def normalise(u):
                x = units[u]
                dve.wait_ge(exp_done, u + 1)
                den = DEN[:, u, :]
                if x["sink"] is not None:
                    do(dve.tensor_tensor(den, den, ES[:, x["sink"], :], ALU.add))
                    do.after()
                do(dve.reciprocal(den, den))
                do.after()
                if x["gate"] is not None:
                    do(dve.tensor_tensor(den, den, G3[:, :, x["gate"]], ALU.mult))
                    do.after()
                p = PR[:, u % 3, :]
                do(dve.tensor_scalar(p[:, 0:P], p[:, 0:P], DEN[:, u, 0:1], None, ALU.mult), probs)
                do(dve.tensor_scalar(p[:, P:TRI], p[:, P:TRI], DEN[:, u, 1:2], None, ALU.mult), probs)

            gates_made = [0]

            def gate(j):
                n = gates_made[0]
                dve.wait_ge(tanh_done, n + 1)
                z = ZS[:, 2 * j:2 * j + 2, :]
                do(dve.scalar_tensor_tensor(z, ZT[:, n % 2, :].rearrange("p (b s) -> p b s", b=2), 1.0, z, ALU.add,
                                            ALU.mult), gated)
                gates_made[0] += 1

            def heads_out(layer, u):
                x = units[u]
                if not (x["last"] and x["q"] % 2):
                    return
                use = f"o{layer}.{x['o']}"
                bank = ps.wait_filled(dve, use)
                do.after()
                dve.wait_ge(gated, 4 * layer + x["o"] // 2 + 1)
                ps.drain(dve.tensor_tensor(OT[:, x["o"], :], bank[:, 0:S], ZS[:, x["o"], :], ALU.mult), use)

            def attention(layer, extra):
                a, b = spans[layer]
                for i in range(a, b + 4):
                    if i < b:
                        mask_scores(i)
                    if a <= i - 1 < b:
                        normalise(i - 1)
                    for what in extra.get(i - a, ()):
                        what()
                    if a <= i - 4 < b:
                        heads_out(layer, i - 4)

            def add_output(layer):
                for t in range(NT):
                    for c in range(2):
                        use = f"y{layer}.{t}.{c}"
                        bank = ps.wait_filled(dve, use)
                        for cc in range(2):
                            ps.wait_drained(dve, f"gate{layer}.{cc}")
                        tmp = (ROT1, ROT2)[c]
                        do.after()
                        ps.drain(dve.tensor_tensor(tmp[:, :], bank[:, :], GATE[:, c * 512:(c + 1) * 512], ALU.mult), use)
                        ps.wait_drained(dve, use)
                        xs = X[:, t, c * 512:(c + 1) * 512]
                        do(dve.tensor_tensor(xs, xs, tmp[:, :], ALU.add), x_new)

            dve.wait_ge(params_in, 32)
            do(dve.tensor_scalar(CTMP[:, :], col("c"), 0.5, None, ALU.mult), cact_half)
            dve.wait_ge(sinks_got, 16)
            do(dve.tensor_scalar(NSINK[:, :], SINK[:, :], -1.0, None, ALU.mult))
            for tile, src, k in ((GBH, "gateb", 0.5), (LGH, "lng", 0.5), (LBH, "lnb", 0.5)):
                do(dve.tensor_scalar(tile[:, :], col(src), k, None, ALU.mult))
            do(dve.tensor_scalar(QKG[:, 0:1], col("qg"), SCALE, None, ALU.mult))
            do(dve.tensor_copy(QKG[:, 1:2], col("kg")), half_cols)
            dve.wait_ge(cact_tanh, 1)
            do(dve.scalar_tensor_tensor(CACT[:, :], CACT[:, :], 1.0, CTMP[:, :], ALU.add, ALU.mult))
            ada(0, 0)
            for t in range(NT):
                stat("n0", t)
            ada(0, 1)
            dve.wait_ge(x_got, 16)
            for t in range(NT):
                hat("n0", t)
            ada(0, 2)
            ada(0, 3)
            modulation(0)
            evict_norm(0)
            rotate("kcks", 0)
            ada(0, 4)
            rotate("kcks", 1)
            rotate("kakw", 0)
            ada(0, 5)
            rotate("kakw", 1)
            do(dve.tensor_scalar(G3[:, :, :], G3[:, :, :], 0.5, 0.5, ALU.mult, ALU.add))
            for t in range(NT):
                ps.wait_drained(dve, f"up.{t}")
            build_u(0)
            build_u(1)
            rotate("qa", 0)
            rotate("qa", 1)
            ada(1, 0)
            rotate("qb", 0)
            rotate("qb", 1)
            ada(1, 1)
            hidden(0)
            hidden_out(0)
            hidden(1)
            hidden_out(1)
            ada(1, 2)

            def compressed_mask():
                m = const("cmpadd").rearrange("p (t c) -> p t c", t=NT).unsqueeze(2)
                m = m.to_broadcast([P, NT, B_HEADS // 2, NC])
                for half in range(2):
                    use = f"cmp.{half}"
                    bank = ps.wait_filled(dve, use)
                    s = bank[:, 0:NT * B_HEADS // 2 * NC].rearrange("p (t h c) -> p t h c", t=NT, h=B_HEADS // 2)
                    dst = CE[:, :, :, :].rearrange("p t (h u) c -> p t u h c", u=2)[:, :, half, :, :]
                    ps.drain(dve.tensor_tensor(dst, s, m, ALU.add), use)
                    ps.wait_drained(dve, use)
                do(dve.tensor_reduce(CM[:, 0, :, :], CE[:, :, :, :], AX.X, ALU.max))
                do.after()
                do(dve.tensor_tensor(CE[:, :, :, :], CE[:, :, :, :],
                                     CM[:, 0, :, :].unsqueeze(3).to_broadcast([P, NT, B_HEADS, NC]), ALU.subtract),
                   cmp_masked)

            def compressed_probs():
                dve.wait_ge(cmp_exp, 1)
                m = const("cmp01").rearrange("p (t c) -> p t c", t=NT).unsqueeze(2).to_broadcast([P, NT, B_HEADS, NC])
                do(dve.tensor_tensor(CE[:, :, :, :], CE[:, :, :, :], m, ALU.mult))
                do.after()
                do(dve.tensor_reduce(CM[:, 1, :, :], CE[:, :, :, :], AX.X, ALU.add))
                do.after()
                do(dve.tensor_tensor(CM[:, 1, :, :], CM[:, 1, :, :],
                                     const("cmpfix").unsqueeze(2).to_broadcast([P, NT, B_HEADS]), ALU.add))
                do.after()
                do(dve.reciprocal(CM[:, 2, :, :], CM[:, 1, :, :]))
                do.after()
                do(dve.tensor_tensor(CM[:, 3, :, :], CM[:, 2, :, :],
                                     G3[:, :, :].rearrange("p t (h b) -> p t h b", b=3)[:, :, :, 0], ALU.mult))
                do.after()
                dve.wait_ge(consts_set, 4)
                do(dve.tensor_tensor(CP[:, :, :, 0:NC], CE[:, :, :, :],
                                     CM[:, 3, :, :].unsqueeze(3).to_broadcast([P, NT, B_HEADS, NC]), ALU.mult), cmp_probs)

            attention(0, {1: [lambda: gate(0)], 2: [lambda: gate(1)], 3: [lambda: ada(1, 3)], 5: [lambda: ada(1, 4)],
                          6: [compressed_mask], 7: [compressed_probs], 9: [lambda: gate(2)], 11: [lambda: gate(3)],
                          13: [lambda: ada(1, 5)]})
            add_output(0)

            for t in range(NT):
                stat("n1", t)
            for t in range(NT):
                hat("n1", t)
            modulation(1)
            evict_norm(1)
            for name, t in rot_order[8:12]:
                rotate(name, t)
            attention(1, {1: [lambda: gate(0)], 2: [lambda: gate(1), lambda: rotate("q1_1", 0)],
                          3: [lambda: rotate("q1_1", 1)], 4: [lambda: rotate("k1_1", 0)], 5: [lambda: rotate("k1_1", 1)],
                          10: [lambda: gate(2)], 12: [lambda: gate(3)]})
            add_output(1)

            for t in range(NT):
                stat("nf", t)
            dve.wait_ge(fing_in, 16)
            for t in range(NT):
                i = powers.index(f"nf_{t}")
                dve.wait_ge(rstds, i + 1)
                do(dve.scalar_tensor_tensor(X[:, t, :], X[:, t, :], RS[:, i, 0:1], FING[:, :], ALU.mult, ALU.mult), x_new)
            do.after()
            for t in range(NT):
                stat("n2", t)
            for t in range(NT):
                hat("n2", t)
            evict_norm(2)
            dve.wait_ge(consts_set, 6)
            for j in range(2):
                ps.wait_drained(dve, f"val.{j}")
                ps.wait_drained(dve, f"cga.{j}")
                do(dve.scalar_tensor_tensor(HB[:, 2 * j:2 * j + 2, CONF_TAPS - 1:],
                                            ZT[:, j, :].rearrange("p (b s) -> p b s", b=2), 1.0,
                                            VALH[:, 2 * j:2 * j + 2, :], ALU.add, ALU.mult))
            do.after()
            taps = {}

            def conf_taps(lo, hi):
                w = col("confw")
                for k in range(lo, hi):
                    for b in range(CB):
                        wk = w[:, b * CONF_TAPS + k:b * CONF_TAPS + k + 1]
                        src = HB[:, b, k:k + S]
                        if k == 0:
                            ins = dve.tensor_scalar(CV[:, b, :], src, wk, col("confb")[:, b:b + 1], ALU.mult, ALU.add)
                        else:
                            do.after(taps[b])
                            ins = dve.scalar_tensor_tensor(CV[:, b, :], src, wk, CV[:, b, :], ALU.mult, ALU.add)
                        last = k == CONF_TAPS - 1 and b == CB - 1
                        taps[b] = do(ins, conv_done if last else None)

            def qk_norm(name, t):
                n = "q_" if name == "q2" else "k_"
                p = powers.index(f"{n}{t}")
                i = 2 * (name == "k2") + t
                use = f"{name}.{t}"
                dve.wait_ge(qk_sq, i + 1)
                do(dve.tensor_reduce(MS[:, p, :], LNH[:, i % 2, :].rearrange("p (h d) -> p h d", h=S_HEADS), AX.X, ALU.add))
                do.after()
                do(dve.tensor_scalar(MS[:, p, :], MS[:, p, :], 1.0 / HD, EPS, ALU.mult, ALU.add), means)
                if name == "q2" or t >= 0:
                    conf_taps(*qk_pieces[i])
                bank = ps.wait_filled(dve, use)
                dve.wait_ge(rstds, p + 1)
                if i >= 2:
                    ps.wait_filled(dve, f"q2.{t}.T")
                ps.drain(dve.tensor_tensor(QR[:, i % 2, :].rearrange("p (h d) -> p h d", h=S_HEADS),
                                           bank[:, :].rearrange("p (h d) -> p h d", h=S_HEADS),
                                           RS[:, p, :].unsqueeze(2).to_broadcast([P, S_HEADS, HD]), ALU.mult), use)

            qk_pieces = [(0, 1), (1, 3), (3, 5), (5, 7)]
            for name in ("q2", "k2"):
                for t in range(NT):
                    qk_norm(name, t)
            conf_taps(7, 13)
            for j in range(2):
                bank = ps.wait_filled(dve, f"scg.{j}")
                ps.wait_drained(dve, f"scx.{j}")
                ps.drain(dve.tensor_tensor(SB[:, 2 * j:2 * j + 2, SC_TAPS - 1:],
                                           bank[:, :].rearrange("p (b s) -> p b s", b=2),
                                           SCX[:, 2 * j:2 * j + 2, :], ALU.mult), f"scg.{j}")
                ps.wait_drained(dve, f"scg.{j}")
            w = col("scw")
            for k in range(SC_TAPS):
                for b in range(CB):
                    wk = w[:, b * SC_TAPS + k:b * SC_TAPS + k + 1]
                    if k == 0:
                        ins = dve.tensor_scalar(SV[:, b, :], SB[:, b, k:k + S], wk, None, ALU.mult)
                    else:
                        do.after(taps[CB + b])
                        ins = dve.scalar_tensor_tensor(SV[:, b, :], SB[:, b, k:k + S], wk, SV[:, b, :], ALU.mult, ALU.add)
                    taps[CB + b] = do(ins)
            do.after()
            for j in range(2):
                bank = ps.wait_filled(dve, f"sbg.{j}")
                sv = SV[:, 2 * j:2 * j + 2, :]
                ps.drain(dve.tensor_tensor(sv, bank[:, :].rearrange("p (b s) -> p b s", b=2), sv, ALU.mult), f"sbg.{j}")
            conf_taps(13, CONF_TAPS)
            for t in range(NT):
                bank = ps.wait_filled(dve, f"ln.{t}")
                p = powers.index(f"ln_{t}")
                do(dve.bn_stats(STAT[:, t, 0:6], bank[:, :]))
                do.after()
                do(dve.bn_aggr(STAT[:, t, 6:8], STAT[:, t, 0:6]))
                do.after()
                do(dve.tensor_scalar(MS[:, p, 0:1], STAT[:, t, 7:8], EPS, None, ALU.add), means)
            for t in range(NT):
                p = powers.index(f"ln_{t}")
                dve.wait_ge(rstds, p + 1)
                ps.drain(dve.tensor_scalar(LNH[:, t, :], tiles[ps.uses[f"ln.{t}"][0]][:, :], STAT[:, t, 6:7],
                                           RS[:, p, 0:1], ALU.subtract, ALU.mult), f"ln.{t}")
            for t in range(NT):
                dve.wait_ge(ln_tanh, t + 1)
                y = LNY[:, :, t * P:(t + 1) * P]
                do(dve.scalar_tensor_tensor(y, ZT[:, t, :].rearrange("p (b s) -> p b s", b=CB), 1.0, y, ALU.add, ALU.mult),
                   ln_done)

            def branch(use, j, gate_block, first, last=False):
                bank = ps.wait_filled(dve, use)
                y = bank[:, :].rearrange("p (b s) -> p b s", b=2)
                g = GT[:, gate_block + 2 * j:gate_block + 2 * j + 2, :]
                m = MT[:, 2 * j:2 * j + 2, :]
                if first:
                    ps.drain(dve.scalar_tensor_tensor(m, g, 1.0, y, ALU.add, ALU.mult), use)
                    return
                tmp = (ROT1, ROT2)[j % 2][:, :].rearrange("p (b s) -> p b s", b=2)
                do.after()
                ps.drain(dve.scalar_tensor_tensor(tmp, g, 1.0, y, ALU.add, ALU.mult), use)
                ps.wait_drained(dve, use)
                do(dve.tensor_tensor(m, m, tmp, ALU.add), merged if last else None)

            def soft_mask(h):
                bank = ps.wait_filled(dve, f"z.{h}")
                dve.wait_ge(soft_ln, h + 1)
                if h >= 3:
                    ps.wait_filled(dve, f"r.{h - 3}")
                e, p = E[:, h % 3, :], PR[:, h % 3, :]
                do(dve.scalar_tensor_tensor(e, bank[:, 0:TRI], 0.0, p, ALU.max, ALU.add))
                do.after()
                do(dve.tensor_tensor(e, e, const("stick01"), ALU.mult), soft_masked)
                ps.drain(dve.tensor_tensor(p, bank[:, 0:TRI], const("stickadd"), ALU.add), f"z.{h}")

            def add_rest(h):
                bank = ps.wait_filled(dve, f"r.{h}")
                ps.wait_drained(dve, f"z.{h}")
                p = PR[:, h % 3, :]
                ps.drain(dve.tensor_tensor(p, bank[:, 0:TRI], p, ALU.add), f"r.{h}")

            for i in range(S_HEADS + 5):
                if i < S_HEADS:
                    soft_mask(i)
                if 0 <= i - 2 < S_HEADS:
                    add_rest(i - 2)
                if i < 4:
                    branch(f"sco.{i}", i, 16, True)
                elif i < 8:
                    branch(f"cfo.{i - 4}", i - 4, 8, False)
                if 0 <= i - 5 < S_HEADS and (i - 5) % 2:
                    o = (i - 5) // 2
                    bank = ps.wait_filled(dve, f"so.{o}")
                    ps.drain(dve.tensor_copy(OT[:, o, :], bank[:, 0:S]), f"so.{o}")
            for j in range(4):
                branch(f"ato.{j}", j, 0, False, True)
            for t in range(NT):
                for c in range(2):
                    use = f"y2.{t}.{c}"
                    bank = ps.wait_filled(dve, use)
                    xs = X[:, t, c * 512:(c + 1) * 512]
                    ps.drain(dve.scalar_tensor_tensor(xs, bank[:, :], 0.5, xs, ALU.mult, ALU.add), use)
            for t in range(NT):
                stat("n3", t)
            for t in range(NT):
                hat("n3", t)
            evict_norm(3)
            for i in range(FB // 2):
                ps.wait_drained(dve, f"fg.{i}")
                bank = ps.wait_filled(dve, f"fu.{i}")
                ps.drain(dve.tensor_tensor(GT[:, 2 * i:2 * i + 2, :], ZT[:, i % 2, :].rearrange("p (b s) -> p b s", b=2),
                                           bank[:, :].rearrange("p (b s) -> p b s", b=2), ALU.mult), f"fu.{i}")
            for n in range(2 * NT):
                bank = ps.wait_filled(dve, f"ff.{n}")
                xs = X[:, n // 2, (n % 2) * 512:(n % 2 + 1) * 512]
                ps.drain(dve.tensor_tensor(xs, bank[:, :], xs, ALU.add), f"ff.{n}")


def constants():
    table, n = const_table()
    out = np.zeros((P, n), np.float32)

    def put(name, a):
        at, w = table[name]
        out[:, at:at + w] = np.asarray(a, np.float32).reshape(P, w)

    put("ident", np.eye(P))
    inv = (np.float32(10000.0) ** (-np.arange(0, HD, 2, dtype=np.float32) / np.float32(HD))).astype(np.float32)
    ang = np.arange(S, dtype=np.float32)[:, None] * inv[None, :]
    c, s = np.cos(ang), np.sin(ang)
    put("ropec", np.concatenate([c, c], 1).reshape(NT, P, HD).transpose(1, 0, 2))
    put("ropes", np.concatenate([-s, s], 1).reshape(NT, P, HD).transpose(1, 0, 2))
    p = np.arange(P)
    diff = np.concatenate([p[:, None] - p[None, :], P + p[:, None] - np.arange(S)[None, :]], 1)
    put("maskc", np.where(diff >= 0, 0.0, NEG))
    put("maskw", np.where((diff >= 0) & (diff < 128), 0.0, NEG))
    tok = np.arange(S).reshape(NT, P).T[:, :, None]
    reach = tok >= CMP_STRIDE * np.arange(NC)[None, None, :] + CMP_LEN - 1
    put("cmpadd", np.where(reach, 0.0, NEG))
    put("cmp01", reach)
    put("cmpfix", ~reach.any(2))
    put("tri", -(p[:, None] >= p[None, :]).astype(np.float32))
    put("negone", -np.ones((P, P)))
    before = np.concatenate([p[:, None] < np.arange(S)[None, :], p[:, None] < p[None, :]], 1)
    put("stick01", before)
    put("stickadd", np.where(before, 0.0, NEG))
    return out


def kernel(**inputs):
    import concourse.bacc as _bacc
    from concourse.bass_utils import run_bass_kernel_spmd as _run

    a = {k: np.asarray(v) for k, v in inputs.items()}
    we = a["w_in_even"][0]
    off = np.cumsum([0, 512, 64, 64, 512, 512, 128, 128, 128, 128, 128, 128, 24, 512])
    qa, ka, va, za, qb, kc, vc, ks, vs, kw, vw, gb, zb = (we[:, off[i]:off[i + 1]] for i in range(13))
    wo = a["w_in_odd"][0]
    w2 = a["w_in_2"][0]
    wi = a["w_ffn_in_2"][0]
    named = {"kcks": np.concatenate([kc, ks, vc, vs], 1), "kakw": np.concatenate([ka, kw, va, vw, gb], 1),
             "qa": qa, "qb": qb, "za": za, "zb": zb, "w1k": a["cmp_w1_k"][0], "w1v": a["cmp_w1_v"][0],
             "q2": w2[:, 0:512], "k2": w2[:, 512:1024], "v2": w2[:, 1024:1536], "val": w2[:, 1536:2048],
             "cga": w2[:, 2048:2560], "scx": w2[:, 2560:3072], "sbg": w2[:, 3072:3584], "scg": w2[:, 3584:4096],
             "sco": a["w_sc_out_2"][0], "cfo": a["w_conf_out_2"][0], "ato": a["w_attn_out_2"][0]}
    for c in range(6):
        named[f"ada0_{c}"] = a["w_ada"][0][:, c * 512:(c + 1) * 512]
        named[f"ada1_{c}"] = a["w_ada"][1][:, c * 512:(c + 1) * 512]
        named[f"g{c}"] = w2[:, 4096 + c * 512:4096 + (c + 1) * 512]
    for c in range(2):
        cc = slice(c * 512, (c + 1) * 512)
        named[f"wo0_{c}"], named[f"wo1_{c}"] = a["w_out_even"][0][:, cc], a["w_out_odd"][0][:, cc]
        named[f"wf{c}"] = a["w_o_2"][0][:, cc]
        for i, n in enumerate("qkvz"):
            named[f"{n}1_{c}"] = wo[:, i * D + c * 512:i * D + (c + 1) * 512]
    for i in range(FB // 2):
        named[f"fi{i}"] = np.concatenate([wi[:, i * 256:(i + 1) * 256], wi[:, D_FF + i * 256:D_FF + (i + 1) * 256]], 1)
    for i in range((FB + 3) // 4):
        named[f"fo{i}"] = a["w_ffn_out_2"][0][i * 512:(i + 1) * 512]
    chunks = chunk_table()
    weights = np.zeros((len(chunks), P, CHUNK), np.float32)
    for n, (name, kb, width) in enumerate(chunks):
        weights[n, :, 0:kb * width] = named[name].reshape(kb, P, width).transpose(1, 0, 2).reshape(P, kb * width)

    def rows(v, n):
        return v.reshape(n, P).T

    def channels(w):
        return w.reshape(w.shape[0], CB, P).transpose(2, 1, 0).reshape(P, -1)

    def pairs(e):
        return e.reshape(16, P).T

    def twice(v):
        return np.concatenate([v, v]).reshape(P, 1)

    w2k = a["cmp_w2_k"][0].reshape(2, P, HD).transpose(1, 0, 2)
    w2v = a["cmp_w2_v"][0].reshape(2, P, HD).transpose(1, 0, 2)
    col_parts = {"c": rows(a["c"][0], KB), "ng0": rows(a["norm_g"][0], KB), "ng1": rows(a["norm_g"][1], KB),
                 "mixg": rows(a["mix_norm_g_2"][0], KB), "ffng": rows(a["ffn_norm_g_2"][0], KB),
                 "gateb": rows(a["gate_b_2"][0].reshape(-1), 24), "confw": channels(a["conf_dw_w_2"][0]),
                 "confb": rows(a["conf_dw_b_2"][0], CB), "lng": rows(a["conf_ln_g_2"][0], CB),
                 "lnb": rows(a["conf_ln_b_2"][0], CB), "scw": channels(a["sc_conv_w_2"][0]),
                 "qg": twice(a["q_norm_g_2"][0]), "kg": twice(a["k_norm_g_2"][0]), "pek": pairs(a["cmp_pe_k"][0]),
                 "pev": pairs(a["cmp_pe_v"][0]), "w2k": np.concatenate([w2k, w2k], 2).reshape(P, 256),
                 "w2v": w2v.reshape(P, 128)}
    table, _ = column_table()
    cols = np.concatenate([col_parts[n] for n in table], 1)
    given = {"weights": weights, "x": a["x"], "consts": constants(), "cols": cols, "b_ada": a["b_ada"],
             "final_g": a["final_g"], "sinks": a["a_sinks"][0]}
    nc = _bacc.Bacc("TRN2", target_bir_lowering=False, num_devices=1)
    arrays, args = {}, []
    for name, v in given.items():
        v = np.ascontiguousarray(v)
        arrays[f"in_{name}_dram"] = v
        args.append(nc.dram_tensor(f"in_{name}_dram", v.shape, mybir.dt.from_np(v.dtype), kind="ExternalInput").ap())
    args.append(nc.dram_tensor("out_0_dram", (1, S, D), F32, kind="ExternalOutput").ap())
    two_blocks_kernel(nc, *args)
    r = _run(nc, [arrays], core_ids=[0])
    return r.results[0]["out_0_dram"]
```

```python
from contextlib import ExitStack

import numpy as np

import concourse.bass as bass
from concourse import mybir

F32 = mybir.dt.float32
F32R = mybir.dt.float32r
ALU = mybir.AluOpType
ACT = mybir.ActivationFunctionType
AX = mybir.AxisListType

P = 128
S = 256
NT = S // P
D = 1024
KB = D // P
HD = 64
HALF = HD // 2
EPS = 1e-6
SCALE = HD ** -0.5
NEG = -1e30
A_HEADS, B_HEADS, B_GROUPS, C_HEADS, S_HEADS = 8, 8, 2, 16, 8
CMP_LEN, CMP_STRIDE, CMP_HID = 32, 16, 256
NC = (S - CMP_LEN) // CMP_STRIDE + 1
D_FF = 2816
FB = D_FF // P
CONF_TAPS, SC_TAPS = 31, 3
CB = 4
PIECE = 2048
RAW_RING = 3
SPLIT_RING = 4
TRI = 384


def piece_table():

    def two(name, kb, width, use):
        return [(name, 0, kb, width, use), (name, 1, kb, width, use)]

    def rows(*names):
        return [p for n in names for p in two(n, KB // 2, 512, "rows")]

    def cols(*names):
        return [p for n in names for p in two(n, KB, 256, "cols")]

    def ada(layer, *cs):
        return [p for c in cs for p in two(f"ada{layer}_{c}", KB // 2, 512, "ada")]

    def between(layer, a, b):
        return [p for pair in zip(ada(layer, a), ada(layer, b)) for p in pair]

    t = between(0, 0, 1) + between(0, 2, 3) + rows("kcks") + two("kakw", KB // 2, 408, "rows")
    t += rows("qa", "qb") + two("w1k", 8, 256, "raw") + two("w1v", 8, 256, "raw")
    t += cols("za", "zb") + ada(0, 4, 5) + ada(1, 1, 0, 3, 2) + rows("wo0_0", "wo0_1")
    t += rows("q1_0", "k1_0", "v1_0") + cols("z1_0") + ada(1, 4) + rows("q1_1", "k1_1", "v1_1") + cols("z1_1")
    t += ada(1, 5) + rows("wo1_0", "wo1_1")
    t += cols("val", "cga") + rows("q2", "k2", "v2") + cols("scx", "scg", "sbg", *(f"g{i}" for i in range(6)))
    t += rows("wf0", "wf1") + two("sco", 4, 512, "raw") + two("cfo", 4, 512, "raw") + two("ato", 4, 512, "raw")
    t += cols(*(f"fi{i}" for i in range(FB // 2)))
    t += [(f"fo{i // 2}", i % 2, 2, 1024, "rows") for i in range(FB // 2)]
    return t


def column_table():
    sizes = [("c", KB), ("ng0", KB), ("ng1", KB), ("mixg", KB), ("ffng", KB), ("gateb", 24),
             ("confw", CB * CONF_TAPS), ("confb", CB), ("lng", CB), ("lnb", CB), ("scw", CB * SC_TAPS),
             ("qg", 1), ("kg", 1), ("pek", 16), ("pev", 16)]
    out, at = {}, 0
    for name, n in sizes:
        out[name] = (at, n)
        at += n
    return out, at


def const_table(late=False):
    sizes = [("tri", P), ("negone", P), ("stick01", TRI), ("stickadd", TRI)] if late else [("ident", P), ("ropec", NT * HD), ("ropes", NT * HD), ("maskc", TRI), ("maskw", TRI),
             ("cmpadd", NT * NC), ("cmp01", NT * NC), ("cmpfix", NT)]
    out, at = {}, 0
    for name, n in sizes:
        out[name] = (at, n)
        at += n
    return out, at


class Psum:

    KINDS = {"proj": (0, 1), "turn": (2, 3), "score": (4, 5), "out": (6, 7)}

    def __init__(self, tiles, filled, drained):
        self.tiles, self.filled, self.drained = tiles, filled, drained
        self.uses, self.n, self.turns = {}, [0] * 8, dict.fromkeys(self.KINDS, 0)

    def open(self, pe, kind, name):
        banks = self.KINDS[kind]
        b = banks[self.turns[kind] % len(banks)]
        self.turns[kind] += 1
        if self.n[b]:
            pe.wait_ge(self.drained[b], self.n[b])
        self.n[b] += 1
        assert name not in self.uses, name
        self.uses[name] = (b, self.n[b])
        return self.tiles[b]

    def fill(self, ins, name):
        ins.then_inc(self.filled[self.uses[name][0]], 1)

    def filled_at(self, name):
        b, n = self.uses[name]
        return self.filled[b], n

    def wait_filled(self, eng, name):
        b, n = self.uses[name]
        eng.wait_ge(self.filled[b], n)
        return self.tiles[b]

    def drain(self, ins, name):
        ins.then_inc(self.drained[self.uses[name][0]], 1)

    def wait_drained(self, eng, name):
        b, n = self.uses[name]
        eng.wait_ge(self.drained[b], n)


class Order:

    def __init__(self, eng, own):
        self.eng, self.own, self.n, self.last = eng, own, {}, None

    def __call__(self, ins, sem=None):
        sem = self.own if sem is None else sem
        ins.then_inc(sem, 1)
        self.n[id(sem)] = self.n.get(id(sem), 0) + 1
        self.last = (sem, self.n[id(sem)])
        return self.last

    def after(self, token=None):
        token = token or self.last
        if token:
            self.eng.wait_ge(*token)


def two_blocks_kernel(nc, weights, x_in, consts_in, late_in, cols_in, bada_in, finalg_in, w2_in, sinks_in, out):
    pieces = piece_table()
    index = {(p[0], p[1]): n for n, p in enumerate(pieces)}
    split = {}
    for n, p in enumerate(pieces):
        if p[4] in ("rows", "cols"):
            split[n] = len(split)
    split_pieces = list(split)
    cols, n_cols = column_table()
    cst, n_cst = const_table()
    cst2, n_cst2 = const_table(late=True)

    with ExitStack() as ctx:
        def sb(name, shape, dt=F32):
            return ctx.enter_context(nc.sbuf_tensor(name, shape, dt))

        def sem(name):
            return ctx.enter_context(nc.semaphore(name))

        RAW = sb("RAW", [P, RAW_RING, PIECE])
        WH, WL = sb("WH", [P, SPLIT_RING, PIECE], F32R), sb("WL", [P, SPLIT_RING, PIECE], F32R)
        X = sb("X", [P, NT, D])
        HH, HL = sb("HH", [P, KB, S], F32R), sb("HL", [P, KB, S], F32R)
        CST, COL = sb("CST", [P, n_cst]), sb("COL", [P, n_cols])
        ONES = sb("ONES", [P, P])
        HALFNEG = sb("HALFNEG", [P, 8])
        GATE = sb("GATE", [P, D])
        SINK, NSINK = sb("SINK", [P, A_HEADS]), sb("NSINK", [P, A_HEADS])
        CACT, CTMP = sb("CACT", [P, KB]), sb("CTMP", [P, KB])
        ADA, MOD = sb("ADA", [P, 2 * KB]), sb("MOD", [P, KB])
        SQ, MS, RS = sb("SQ", [P, 16]), sb("MS", [P, 16, 8]), sb("RS", [P, 16, 8])
        ROT1, ROT2 = sb("ROT1", [P, 512]), sb("ROT2", [P, 512])
        QR = sb("QR", [P, 2, 512])
        G3 = sb("G3", [P, NT, 24])
        ZT = sb("ZT", [P, 2, 512])
        E, PR, PT = sb("E", [P, 2, TRI]), sb("PR", [P, 3, TRI]), sb("PT", [P, 2, TRI])
        n_units = A_HEADS + 2 * B_HEADS + C_HEADS
        NM, DEN, ES = sb("NM", [P, n_units, 2]), sb("DEN", [P, n_units, 2]), sb("ES", [P, A_HEADS, 2])
        STAT = sb("STAT", [P, NT, 8])
        GBH, LGH, LBH, QKG = sb("GBH", [P, 24]), sb("LGH", [P, CB]), sb("LBH", [P, CB]), sb("QKG", [P, 2])

        def place(stack, *wanted):
            return [stack.enter_context(nc.sbuf_tensor(n, shape, dt)) for n, shape, dt in wanted]

        with ExitStack() as early:
            QT, KT, V, ZS, BIG = place(early, ("QT", [P, KB, S], F32), ("KT", [P, KB, S], F32), ("V", [P, NT, D], F32),
                                       ("ZS", [P, KB, S], F32), ("BIG", [P, 24 * S], F32))
        AH, AL, _ = place(ctx, ("AH", [P, FB, S], F32R), ("AL", [P, FB, S], F32R),
                          ("AREST", [P, (4 * KB + 24 - 2 * FB) * S], F32))
        with ExitStack() as early:
            UP, CPT = place(early, ("UP", [P, 4, P], F32), ("CPT", [P, 2, S], F32))
        HB, = place(ctx, ("HB", [P, CB, CONF_TAPS - 1 + S], F32))

        def carve(area, *shapes):
            out_, at = [], 0
            names = "abcd"
            for shape in shapes:
                n = int(np.prod(shape))
                view = area[:, at:at + n]
                dims = " ".join(names[:len(shape)])
                sizes = {names[i]: shape[i] for i in range(len(shape) - 1)}
                out_.append(view.rearrange(f"p ({dims}) -> p {dims}", **sizes) if len(shape) > 1 else view)
                at += n
            assert at <= area.shape[1], (at, area.shape)
            return out_

        v_free = 5 * HD
        CP, HX, HQ, HTH = carve(V[:, 0, v_free:], (NT, B_HEADS, 32), (4 * NC,), (4 * NC,), (4 * NC,))
        HID4, HID, KCT = carve(V[:, 1, v_free:], (2, 2, 4, 32), (2, 4 * NC), (2, NC))
        CE, = carve(KT[:, 5:KB, :].rearrange("p k s -> p (k s)"), (NT, B_HEADS, NC))
        VCM, CM = carve(BIG[:, 4 * D + NT * 7 * 2 * HD:], (2, HD), (4, NT, B_HEADS))
        U, = carve(ZS[:, 0:4, :].rearrange("p k s -> p (k s)"), (4, 16, NC))
        VCD, = carve(ZS[:, 4:6, :].rearrange("p k s -> p (k s)"), (NT, 2, 2, HD))
        W2 = ZS[:, 6:8, :].rearrange("p k s -> p (k s)")[:, 0:384]
        W2K, W2V = W2[:, 0:256], W2[:, 256:384]
        OS = GATE[:, :].rearrange("p (b s) -> p b s", b=CB)
        CST2 = CST[:, cst["ropec"][0]:cst["ropec"][0] + n_cst2]
        sb_width = SC_TAPS - 1 + S
        SB = BIG[:, 24 * S - CB * sb_width:].rearrange("p (b s) -> p b s", b=CB)
        ACC = BIG[:, 0:3 * D]
        FING = BIG[:, 3 * D:4 * D]
        KR = BIG[:, 4 * D:4 * D + NT * 7 * 2 * HD].rearrange("p (t h d) -> p t h d", t=NT, h=7)
        GT = BIG[:, :].rearrange("p (k s) -> p k s", k=24)
        XH = KT[:, :, :].rearrange("p k s -> p (k s)").rearrange("p (t d) -> p t d", t=NT)
        VALH, SCX = ZS, OS
        STICK = [E[:, 0, :], E[:, 1, :], QR[:, 0, 0:TRI]]
        CV, SV = QT[:, CB:2 * CB, :], KT[:, CB:2 * CB, :]
        LNH, LNY = V[:, :, 512:1024], ZS[:, CB:2 * CB, :]
        tiles = [ctx.enter_context(nc.psum_tensor(f"bank{i}", [P, 512], F32)) for i in range(8)]
        ps = Psum(tiles, [sem(f"filled{i}") for i in range(8)], [sem(f"drained{i}") for i in range(8)])

        def merged_block(j):
            return QT[:, CB + 2 * j:CB + 2 * j + 2, :] if j < 2 else ZS[:, 2 * j - 4:2 * j - 2, :]

        params_in, sinks_got, bias_in, fing_in, x_got = (sem("params_in"), sem("sinks_got"), sem("bias_in"),
                                                         sem("fing_in"), sem("x_got"))
        w2_got = sem("w2_got")
        late_got, cols_got = sem("late_got"), sem("cols_got")
        raw_in = [sem(f"raw_in{r}") for r in range(RAW_RING)]
        placed_in = [sem(f"placed_in{i}") for i in range(3)]
        high_done, low_done, piece_read = sem("high_done"), sem("low_done"), sem("piece_read")
        ht_high, ht_low = sem("ht_high"), sem("ht_low")
        ot_high, ot_low, mt_high, mt_low = sem("ot_high"), sem("ot_low"), sem("mt_high"), sem("mt_low")
        ff_high, ff_low, late_set, ada_read = sem("ff_high"), sem("ff_low"), sem("late_set"), sem("ada_read")
        dve_step, act_step = sem("dve_step"), sem("act_step")
        consts_set, acc_clear = sem("consts_set"), sem("acc_clear")
        cact_half, cact_tanh, mod_ready = sem("cact_half"), sem("cact_tanh"), sem("mod_ready")
        cact_ready = sem("cact_ready")
        squares, means, rstds, x_hat, x_new = sem("squares"), sem("means"), sem("rstds"), sem("x_hat"), sem("x_new")
        v_copied, roped = sem("v_copied"), sem("roped")
        u_built, hid_in, hid_tanh, hid_done = sem("u_built"), sem("hid_in"), sem("hid_tanh"), sem("hid_done")
        cmp_masked, cmp_exp, cmp_probs = sem("cmp_masked"), sem("cmp_exp"), sem("cmp_probs")
        masked, exp_done, probs, pv_done = sem("masked"), sem("exp_done"), sem("probs"), sem("pv_done")
        tanh_done, gated = sem("tanh_done"), sem("gated")
        qk_sq, half_cols = sem("qk_sq"), sem("half_cols")
        conv_done, ln_tanh, ln_done = (sem("conv_done"), sem("ln_tanh"),
                                                        sem("ln_done"))
        soft_ln, soft_masked, stick_p = sem("soft_ln"), sem("soft_masked"), sem("stick_p")
        merged, stored = sem("merged"), sem("stored")

        def const(name):
            if name in cst2:
                a, n = cst2[name]
                return CST2[:, a:a + n]
            a, n = cst[name]
            return CST[:, a:a + n]

        def col(name):
            a, n = cols[name]
            return COL[:, a:a + n]

        areas = [("ada0_1", 0, QT), ("ada0_1", 1, V), ("ada0_3", 0, ZS)]
        placed = {index[(name, half)]: t[:, :, :].rearrange("p a b -> p (a b)") for name, half, t in areas}
        ring = [n for n in range(len(pieces)) if n not in placed]
        slot = {n: i for i, n in enumerate(ring)}

        def raw(name, half):
            n = index[(name, half)]
            _, _, kb, w, _ = pieces[n]
            if n in placed:
                return placed[n][:, :].rearrange("p (k c) -> p k c", k=kb)
            return RAW[:, slot[n] % RAW_RING, 0:kb * w].rearrange("p (k c) -> p k c", k=kb)

        def wait_raw(eng, name, half):
            n = index[(name, half)]
            if n in placed:
                eng.wait_ge(placed_in[list(placed).index(n)], 16)
            else:
                eng.wait_ge(raw_in[slot[n] % RAW_RING], 16 * (slot[n] // RAW_RING + 1))

        def parts(name, half):
            n = index[(name, half)]
            _, _, kb, w, _ = pieces[n]
            s = split[n] % SPLIT_RING
            return [t[:, s, 0:kb * w].rearrange("p (k c) -> p k c", k=kb) for t in (WH, WL)]

        def wait_parts(eng, name, half):
            eng.wait_ge(low_done, split[index[(name, half)]] + 1)

        def high_step(layer, o):
            last = 2 * o + 1 if layer == 1 or o < A_HEADS // 2 else A_HEADS + 4 * (o - A_HEADS // 2) + 3
            return max(last + 5, 13)

        def past_columns(fence, make, at):
            def step(k):
                fence[0] = FENCES["columns"]
                make(first_split("wo0_0") + k)
            return {at + k: [lambda k=k: step(k)] for k in range(1, 5)}

        readers = {}
        reads = [0]

        def first_split(name):
            return split[index[(name, 0)]]

        FENCES = {"start": first_split("za"), "hidden": first_split("wo0_0"), "columns": first_split("fi0"),
                  "branches": len(split)}

        ident = const("ident")

        def unit(q, k, v, mask, o, first, last, sink=None, gate=None):
            return dict(q=q, k=k, v=v, mask=mask, o=o, first=first, last=last, sink=sink, gate=gate)

        even, odd = [], []
        for h in range(A_HEADS):
            even.append(unit(h, 2, 2, "maskw", h // 2, True, True, sink=h))
        for h in range(B_HEADS):
            g = h // (B_HEADS // B_GROUPS)
            even.append(unit(A_HEADS + h, g, g, "maskc", 4 + h // 2, False, False, gate=3 * h + 1))
            even.append(unit(A_HEADS + h, 3 + g, 3 + g, "maskc", 4 + h // 2, False, True, gate=3 * h + 2))
        for h in range(C_HEADS):
            odd.append(unit(h, None, h, "maskc", h // 2, True, True))
        units = even + odd
        ada_names = [f"ada{l}_{c}" for l, c in ((0, 0), (0, 2), (0, 4), (0, 5), (1, 0), (1, 2), (1, 4), (1, 5))]
        ada_pieces = [(n, half) for n in ada_names for half in range(2)]
        powers = [f"{n}_{t}" for n in ("n0", "n1") for t in range(NT)]
        powers += [f"{n}_{t}" for t in range(NT) for n in ("nf", "n2")]
        powers += [f"{n}_{t}" for n in ("q", "k", "ln", "n3") for t in range(NT)]
        rot_order = [("kcks", 0), ("kcks", 1), ("kakw", 0), ("kakw", 1), ("qa", 0), ("qa", 1), ("qb", 0), ("qb", 1)]
        rot_order += [(f"{n}1_{g}", t) for g in range(2) for n in "qk" for t in range(NT)]
        rot_index = {r: n for n, r in enumerate(rot_order)}

        spans = ((0, len(even)), (len(even), len(units)))
        pv_at, stick_pv_at, pv_count = {}, {}, [0]

        block = ctx.enter_context(nc.Block())

        @block.tensor
        def _(pe):
            def product(out_, w, x, start, stop, **more):
                pe.matmul(out_, lhsT=w[0], rhs=x[0], start=start, stop=False, **more)
                pe.matmul(out_, lhsT=w[0], rhs=x[1], start=False, stop=False, **more)
                return pe.matmul(out_, lhsT=w[1], rhs=x[0], start=False, stop=stop, **more)

            def mark_read(mm, name, half):
                mm.then_inc(piece_read, 1)
                reads[0] += 1
                readers[index[(name, half)]] = (piece_read, reads[0])

            def by_tokens(name, t, width=512, use=None):
                use = use or f"{name}.{t}"
                bank = ps.open(pe, "proj", use)
                for half in range(2):
                    wait_parts(pe, name, half)
                    wh, wl = parts(name, half)
                    for k in range(KB // 2):
                        kk = half * KB // 2 + k
                        mm = product(bank[:, 0:width], [h[:, kk, t * P:(t + 1) * P] for h in (HH, HL)],
                                     [wh[:, k, 0:width], wl[:, k, 0:width]], kk == 0, kk == KB - 1)
                    if half == 0 and t == NT - 1:
                        mark_read(mm, name, 0)
                ps.fill(mm, use)
                if t == NT - 1:
                    readers[index[(name, 1)]] = ps.filled_at(use)

            def by_features(name, j, use=None):
                wait_parts(pe, name, j)
                w = parts(name, j)
                use = use or f"{name}.{j}"
                bank = ps.open(pe, "proj", use)
                for b in range(2):
                    for k in range(KB):
                        mm = product(bank[:, b * S:(b + 1) * S], [part_[:, k, b * P:(b + 1) * P] for part_ in w],
                                     [HH[:, k, :], HL[:, k, :]], k == 0, k == KB - 1)
                ps.fill(mm, use)
                readers[index[(name, j)]] = ps.filled_at(use)

            def branch(name, j, src):
                if j % 2 == 0:
                    wait_raw(pe, name, j // 2)
                w = raw(name, j // 2)
                use = f"{name}.{j}"
                bank = ps.open(pe, "proj", use)
                for b in range(2):
                    f = (2 * (j % 2) + b) * P
                    for k in range(CB):
                        mm = pe.matmul(bank[:, b * S:(b + 1) * S], lhsT=w[:, k, f:f + P], rhs=src[:, k, :],
                                       start=(k == 0), stop=(k == CB - 1))
                ps.fill(mm, use)
                if j % 2:
                    readers[index[(name, j // 2)]] = ps.filled_at(use)

            def turn(use, blocks, waits=()):
                bank = ps.open(pe, "turn", use)
                for sem_, n in waits:
                    pe.wait_ge(sem_, n)
                for j, src in enumerate(blocks):
                    mm = pe.transpose(bank[:, j * P:(j + 1) * P], src, ident)
                ps.fill(mm, use)

            def norm(n, hat):
                for t in range(NT):
                    if t == 1 and n < 2:
                        conditioning(n)
                    for half in range(2):
                        turn(f"n{n}.{t}.{half}", [XH[:, t, (4 * half + j) * P:(4 * half + j + 1) * P] for j in range(4)],
                             [(x_hat, hat + t + 1)])

            def normed(n, t=NT - 1):
                pe.wait_ge(ht_low, 4 * n + 2 * (t + 1))

            def conditioning_row(layer, c):
                use = f"cols{layer}.{c}"
                bank = ps.open(pe, "proj", use)
                for half in range(2):
                    name = f"ada{layer}_{c}"
                    wait_raw(pe, name, half)
                    w = raw(name, half)
                    for k in range(KB // 2):
                        kk = half * KB // 2 + k
                        mm = pe.matmul(bank[0:1, :], lhsT=CACT[:, kk:kk + 1], rhs=w[:, k, :],
                                       start=(kk == 0), stop=(kk == KB - 1))
                    if half:
                        ps.fill(mm, use)
                        readers[index[(name, half)]] = ps.filled_at(use)
                    else:
                        mark_read(mm, name, half)

            def conditioning(layer):
                pe.wait_ge(ada_read, 8 * layer + 4)
                for c in (1, 3):
                    ps.wait_drained(pe, f"cols{layer}.{c}")
                bank = ps.open(pe, "proj", f"ada{layer}")
                for j in range(2 * KB):
                    mm = pe.matmul(bank[:, j:j + 1], lhsT=ACC[:, j * P:(j + 1) * P], rhs=ONES[:, 0:1],
                                   start=True, stop=True)
                ps.fill(mm, f"ada{layer}")

            def gate_rows(layer):
                pe.wait_ge(ada_read, 8 * layer + 8)
                for c in range(2):
                    bank = ps.open(pe, "proj", f"gate{layer}.{c}")
                    mm = pe.matmul(bank[:, :], lhsT=ONES[:, :], rhs=ACC[:, (4 + c) * 512:(5 + c) * 512],
                                   start=True, stop=True)
                    ps.fill(mm, f"gate{layer}.{c}")

            def key_turns():
                items = [(h, t) for h in range(2, 7) for t in range(NT)]
                for n in range(0, len(items), 4):
                    turn(f"kt.{n // 4}", [KR[:, t, h, :] for h, t in items[n:n + 4]], [(roped, 4)])

            def pair_turn(t):
                pe.wait_ge(v_copied, t + 1)
                turn(f"up.{t}", [KR[:, t, 0, :], KR[:, t, 1, :], VCD[:, t, 0, :, :].rearrange("p a d -> p (a d)"),
                                 VCD[:, t, 1, :, :].rearrange("p a d -> p (a d)")], [(roped, t + 1)])

            def head_turn(name, t):
                i = rot_index[(name, t)]
                turn(f"{name}.{t}.T", [QR[:, i % 2, j * P:(j + 1) * P] for j in range(4)], [(roped, i + 1)])

            def half_of(h, tile, blk, a, b):
                r = slice(HD * (h % 2), HD * (h % 2) + HD)
                return tile[r, blk, a:b]

            def scores(u):
                x = units[u]
                q, k = x["q"], x["k"]
                kb = q // 2 if k is None else k
                bank = ps.open(pe, "score", f"s.{u}")
                pe.matmul(bank[:, 0:P], lhsT=half_of(q, QT, q // 2, 0, P), rhs=half_of(q, KT, kb, 0, P),
                          start=True, stop=True)
                mm = pe.matmul(bank[:, P:TRI], lhsT=half_of(q, QT, q // 2, P, S), rhs=half_of(q, KT, kb, 0, S),
                               start=True, stop=True)
                ps.fill(mm, f"s.{u}")

            def probs_turn(u):
                p = PR[:, u % 3, :]
                turn(f"pt.{u}", [p[:, j * P:(j + 1) * P] for j in (0, 1, 2)], [(probs, 2 * u + 2)])

            def weigh(u, base):
                x = units[u]
                q, v, layer = x["q"], x["v"], base
                use = f"o{layer}.{x['o']}"
                r = slice(HD * (q % 2), HD * (q % 2) + HD)
                if x["first"] and q % 2 == 0 or (x["gate"] is not None and not x["last"] and q % 2 == 0):
                    ps.open(pe, "out", use)
                bank = tiles[ps.uses[use][0]]
                started = False
                if x["gate"] is not None and not x["last"]:
                    h = q - A_HEADS
                    ps.wait_drained(pe, "cmpT")
                    rows = slice(32 * (h % 4), 32 * (h % 4) + 32)
                    pe.matmul(bank[r, 0:S], lhsT=VCM[rows, h // 4, :], rhs=CPT[rows, h // 4, :],
                              start=True, stop=False)
                    started = True
                ps.wait_drained(pe, f"pt.{u}")
                pt = PT[:, u % 2, :]
                pe.matmul(bank[r, 0:S], lhsT=V[:, 0, v * HD:(v + 1) * HD], rhs=pt[:, 0:S],
                          start=(x["first"] and not started), stop=False)
                mm = pe.matmul(bank[r, P:S], lhsT=V[:, 1, v * HD:(v + 1) * HD], rhs=pt[:, S:TRI],
                               start=False, stop=x["last"])
                if x["last"] and q % 2 == 1:
                    ps.fill(mm, use)
                    pv_at[u] = None
                else:
                    mm.then_inc(pv_done, 1)
                    pv_at[u] = pv_count[0] = pv_count[0] + 1

            def second_half():
                for use in ("q1_1.0.T", "q1_1.1.T", "k1_1.0.T", "k1_1.1.T", "v1_1.0", "v1_1.1"):
                    ps.wait_drained(pe, use)

            def attention(layer, extra):
                a, b = spans[layer]
                for i in range(a, b + 3):
                    if layer == 1 and i - a == KB:
                        second_half()
                    if i < b:
                        scores(i)
                    for what in extra.get(i - a, ()):
                        what()
                    if a <= i - 2 < b:
                        probs_turn(i - 2)
                    if a <= i - 3 < b:
                        weigh(i - 3, layer)

            def output(layer):
                for t in range(NT):
                    for c in range(2):
                        by_tokens(f"wo{layer}_{c}" if layer < 2 else f"wf{c}", t, use=f"y{layer}.{t}.{c}")

            def compress_in(kv):
                name = ("w1k", "w1v")[kv]
                pe.wait_ge(u_built, 2 * kv + 2)
                bank = ps.open(pe, "proj", f"hid.{kv}")
                for half in range(2):
                    wait_raw(pe, name, half)
                for hb in range(2):
                    for j in range(16):
                        w = raw(name, j // 8)
                        mm = pe.matmul(bank[:, hb * 2 * NC:(hb + 1) * 2 * NC], lhsT=w[:, j % 8, hb * P:(hb + 1) * P],
                                       rhs=U[:, 2 * kv:2 * kv + 2, j, :], start=(j == 0), stop=(j == 15))
                        if hb == 1 and j == 7:
                            mark_read(mm, name, 0)
                ps.fill(mm, f"hid.{kv}")
                readers[index[(name, 1)]] = ps.filled_at(f"hid.{kv}")

            def compress_out():
                pe.wait_ge(w2_got, 16)
                pe.wait_ge(hid_done, 1)
                bank = ps.open(pe, "proj", "kc2")
                for hb in range(2):
                    mm = pe.matmul(bank[:, 0:2 * NC], lhsT=W2K[:, hb * P:(hb + 1) * P],
                                   rhs=HID[:, 0, hb * 2 * NC:(hb + 1) * 2 * NC], start=(hb == 0), stop=(hb == 1))
                ps.fill(mm, "kc2")
                pe.wait_ge(hid_done, 3)
                bank = ps.open(pe, "proj", "vc2")
                for g in range(2):
                    for hb in range(2):
                        mm = pe.matmul(bank[:, g * HD:(g + 1) * HD],
                                       lhsT=HID4[:, hb, g, :, :].rearrange("p a c -> p (a c)"),
                                       rhs=W2V[:, hb * HD:(hb + 1) * HD], start=(hb == 0), stop=(hb == 1))
                ps.fill(mm, "vc2")

            def compressed_scores():
                ps.wait_drained(pe, "kc2")
                ps.wait_drained(pe, "qb.0.T")
                ps.wait_drained(pe, "qb.1.T")
                for half in range(2):
                    bank = ps.open(pe, "proj", f"cmp.{half}")
                    r = slice(HD * half, HD * half + HD)
                    for t in range(NT):
                        for j in range(B_HEADS // 2):
                            a = (t * (B_HEADS // 2) + j) * NC
                            mm = pe.matmul(bank[:, a:a + NC], lhsT=QT[r, 4 + j, t * P:(t + 1) * P],
                                           rhs=KCT[r, j // 2, :], start=True, stop=True)
                    ps.fill(mm, f"cmp.{half}")

            def compressed_turn():
                ps.wait_drained(pe, "vc2")
                turn("cmpT", [CP[:, t, 4 * g:4 * g + 4, :].rearrange("p h c -> p (h c)")
                              for g in range(2) for t in range(NT)], [(cmp_probs, 1)])

            pe.wait_ge(consts_set, 2)

            pe.wait_ge(cact_ready, 1)
            conditioning_row(0, 1)
            conditioning_row(0, 3)
            pe.wait_ge(params_in, 16)
            norm(0, 0)
            normed(0)
            turns = {1: lambda: pair_turn(0), 2: lambda: pair_turn(1), 4: key_turns, 5: lambda: head_turn("qa", 0),
                     6: lambda: head_turn("qa", 1), 7: lambda: head_turn("qb", 0)}
            for n, (name, t) in enumerate(rot_order[:8]):
                by_tokens(name, t, 408 if name == "kakw" else 512)
                if n in turns:
                    turns[n]()
            compress_in(0)
            head_turn("qb", 1)
            compress_in(1)
            for n in range(3):
                ps.wait_drained(pe, f"kt.{n}")
            for t in range(NT):
                ps.wait_drained(pe, f"qa.{t}.T")
            attention(0, {0: [lambda: by_features("za", 0)], 1: [lambda: by_features("za", 1)], 3: [compress_out],
                          5: [compressed_scores], 8: [compressed_turn, lambda: by_features("zb", 0)],
                          10: [lambda: by_features("zb", 1)], 7: [lambda: gate_rows(0)],
                          9: [lambda: conditioning_row(1, 1)], 12: [lambda: conditioning_row(1, 3)]})
            pe.wait_ge(ot_low, KB)
            output(0)

            norm(1, 2)
            normed(1)
            by_tokens("q1_0", 0)
            by_tokens("q1_0", 1)
            by_tokens("k1_0", 0)
            head_turn("q1_0", 0)
            by_tokens("k1_0", 1)
            head_turn("q1_0", 1)
            by_tokens("v1_0", 0)
            head_turn("k1_0", 0)
            by_tokens("v1_0", 1)
            head_turn("k1_0", 1)
            for use in ("q1_0.0.T", "q1_0.1.T", "k1_0.0.T", "k1_0.1.T", "v1_0.0", "v1_0.1"):
                ps.wait_drained(pe, use)

            attention(1, {0: [lambda: by_features("z1_0", 0)], 1: [lambda: by_features("z1_0", 1)],
                          2: [lambda: by_tokens("q1_1", 0)], 3: [lambda: by_tokens("q1_1", 1)],
                          4: [lambda: by_tokens("k1_1", 0), lambda: head_turn("q1_1", 0)],
                          5: [lambda: by_tokens("k1_1", 1), lambda: head_turn("q1_1", 1)],
                          6: [lambda: by_tokens("v1_1", 0), lambda: head_turn("k1_1", 0)],
                          7: [lambda: by_tokens("v1_1", 1), lambda: head_turn("k1_1", 1)],
                          9: [lambda: by_features("z1_1", 0)], 11: [lambda: by_features("z1_1", 1)]})
            gate_rows(1)
            pe.wait_ge(ot_low, 2 * KB)
            output(1)

            norm(2, 4)
            normed(2)
            for name in ("val", "cga"):
                by_features(name, 0)
                by_features(name, 1)

            def qk_turn(name, t):
                i = 2 * (name == "k2") + t
                turn(f"{name}.{t}.T", [QR[:, i % 2, j * P:(j + 1) * P] for j in range(4)], [])

            by_tokens("q2", 0)
            by_tokens("q2", 1)
            ps.wait_drained(pe, "q2.0")
            qk_turn("q2", 0)
            by_tokens("k2", 0)
            ps.wait_drained(pe, "q2.1")
            qk_turn("q2", 1)
            by_tokens("k2", 1)
            ps.wait_drained(pe, "k2.0")
            qk_turn("k2", 0)
            by_tokens("v2", 0)
            ps.wait_drained(pe, "k2.1")
            qk_turn("k2", 1)
            by_tokens("v2", 1)
            for name in ("scx", "scg", "sbg"):
                by_features(name, 0)
                by_features(name, 1)
            for g in range(6):
                by_features(f"g{g}", 0)
                if g == 5:
                    pe.wait_ge(conv_done, 1)
                    for t in range(NT):
                        turn(f"ln.{t}", [CV[:, b, t * P:(t + 1) * P] for b in range(CB)])
                by_features(f"g{g}", 1)
            pe.wait_ge(late_got, 16)
            for t in range(NT):
                ps.wait_drained(pe, f"ln.{t}")
                turn(f"lnT.{t}", [LNH[:, t, b * P:(b + 1) * P] for b in range(CB)])

            def stick_scores(h):
                bank = ps.open(pe, "score", f"z.{h}")
                pe.matmul(bank[:, 0:S], lhsT=half_of(h, KT, h // 2, 0, P), rhs=half_of(h, QT, h // 2, 0, S),
                          start=True, stop=True)
                mm = pe.matmul(bank[:, S:TRI], lhsT=half_of(h, KT, h // 2, P, S), rhs=half_of(h, QT, h // 2, P, S),
                               start=True, stop=True)
                ps.fill(mm, f"z.{h}")

            def stick_rest(h):
                bank = ps.open(pe, "turn", f"r.{h}")
                pe.wait_ge(soft_masked, h + 1)
                l = STICK[h % 3]
                pe.matmul(bank[:, 0:S], lhsT=const("tri"), rhs=l[:, 0:S], start=True, stop=False)
                pe.matmul(bank[:, P:S], lhsT=const("negone"), rhs=l[:, S:TRI], start=False, stop=True)
                mm = pe.matmul(bank[:, S:TRI], lhsT=const("tri"), rhs=l[:, S:TRI], start=True, stop=True,
                               skip_group_check=True)
                ps.fill(mm, f"r.{h}")

            def stick_weigh(h):
                use = f"so.{h // 2}"
                if h % 2 == 0:
                    ps.open(pe, "out", use)
                bank = tiles[ps.uses[use][0]]
                r = slice(HD * (h % 2), HD * (h % 2) + HD)
                pe.wait_ge(stick_p, h + 1)
                pt = PT[:, h % 2, :]
                pe.matmul(bank[r, 0:S], lhsT=V[:, 0, h * HD:(h + 1) * HD], rhs=pt[:, 0:S], start=True, stop=False)
                mm = pe.matmul(bank[r, P:S], lhsT=V[:, 1, h * HD:(h + 1) * HD], rhs=pt[:, S:TRI],
                               start=False, stop=True)
                if h % 2:
                    ps.fill(mm, use)
                else:
                    mm.then_inc(pv_done, 1)
                    pv_count[0] += 1
                    stick_pv_at[h] = pv_count[0]

            for name, n in (("q2.0.T", 0), ("q2.1.T", 0), ("k2.0.T", 0), ("k2.1.T", 0), ("v2.0", 0), ("v2.1", 0)):
                ps.wait_drained(pe, name)
            for j in range(2):
                ps.wait_drained(pe, f"sbg.{j}")
            for i in range(S_HEADS + 4):
                if i < S_HEADS:
                    stick_scores(i)
                if i < 4:
                    branch("sco", i, SV)
                elif i < 8:
                    pe.wait_ge(ln_done, NT)
                    branch("cfo", i - 4, LNY)
                if 0 <= i - 2 < S_HEADS:
                    stick_rest(i - 2)
                if 0 <= i - 4 < S_HEADS:
                    stick_weigh(i - 4)
            for o in range(4):
                ps.wait_drained(pe, f"so.{o}")
            for j in range(4):
                branch("ato", j, OS)
            pe.wait_ge(mt_low, 4)
            output(2)
            norm(3, 6)
            normed(3)
            for i in range(FB // 2):
                by_features(f"fi{i}", 0, use=f"fg.{i}")
                by_features(f"fi{i}", 1, use=f"fu.{i}")
            banks = [ps.open(pe, kind, f"ff.{n}") for n, kind in enumerate(("score", "score", "out", "out"))]
            for i in range(FB // 2):
                name, half = f"fo{i // 2}", i % 2
                wait_parts(pe, name, half)
                wh, wl = parts(name, half)
                pe.wait_ge(ff_low, i + 1)
                last = i == FB // 2 - 1
                order = [(k, t, c) for k in range(2) for t in range(NT) for c in range(2)]
                if last:
                    order = [(k, t, c) for t in range(NT) for c in range(2) for k in range(2)]
                for k, t, c in order:
                    kk = 2 * i + k
                    mm = product(banks[2 * t + c][:, :], [a[:, kk, t * P:(t + 1) * P] for a in (AH, AL)],
                                 [w[:, k, c * 512:(c + 1) * 512] for w in (wh, wl)], kk == 0, kk == FB - 1)
                    if kk == FB - 1:
                        ps.fill(mm, f"ff.{2 * t + c}")
                if not last:
                    mark_read(mm, name, half)

        @block.sync
        def _(sp):
            sp.dma_start(COL[:, :], cols_in).then_inc(cols_got, 16)
            for n, (name, half, kb, width, use) in enumerate(pieces):
                if n in placed:
                    sp.dma_start(placed[n], weights[n, :, :]).then_inc(placed_in[list(placed).index(n)], 16)
                    continue
                if slot[n] >= RAW_RING:
                    old = ring[slot[n] - RAW_RING]
                    name2, half2, _, _, use2 = pieces[old]
                    if use2 in ("rows", "cols"):
                        sp.wait_ge(low_done, split[old] + 1)
                    elif old in readers:
                        sp.wait_ge(*readers[old])
                    else:
                        sp.wait_ge(ada_read, ada_pieces.index((name2, half2)) + 1)
                sp.dma_start(RAW[:, slot[n] % RAW_RING, 0:kb * width], weights[n, :, 0:kb * width]).then_inc(
                    raw_in[slot[n] % RAW_RING], 16)
            for t in range(NT):
                for c in range(2):
                    ps.wait_drained(sp, f"ff.{2 * t + c}")
                sp.dma_start(out[0, t * P:(t + 1) * P, :], X[:, t, :]).then_inc(stored, 16)
            sp.wait_ge(stored, 16 * NT)

        @block.gpsimd
        def _(pool):
            pool.memset(ACC[:, :], 0.0).then_inc(acc_clear, 1)
            pool.wait_ge(acc_clear, 1)
            pool.dma_start(ACC[0:1, :], bada_in[0:1, :]).then_inc(bias_in, 16)
            pool.memset(ONES[:, :], 1.0).then_inc(consts_set, 1)
            pool.memset(HALFNEG[:, :], -0.5).then_inc(consts_set, 1)
            pool.dma_start(CST[:, :], consts_in).then_inc(params_in, 16)
            pool.dma_start(SINK[:, :], sinks_in.partition_broadcast(P)).then_inc(sinks_got, 16)
            pool.dma_start(FING[:, :], finalg_in.partition_broadcast(P)).then_inc(fing_in, 16)
            pool.wait_ge(consts_set, 2)
            for n, name in enumerate(powers):
                if name == "n1_0":
                    ps.wait_filled(pool, "cols0.3")
                    pool.memset(CP[:, :, :, :], 0.0).then_inc(consts_set, 1)
                    pool.memset(HID4[:, :, :, :, :], 0.0).then_inc(consts_set, 1)
                    pool.dma_start(W2, w2_in).then_inc(w2_got, 16)
                    ps.wait_filled(pool, "gate0.0")
                    ps.wait_filled(pool, "gate0.1")
                    pool.memset(ACC[:, :], 0.0).then_inc(acc_clear, 1)
                    pool.wait_ge(acc_clear, 2)
                    pool.dma_start(ACC[0:1, :], bada_in[1:2, :]).then_inc(bias_in, 16)
                w = S_HEADS if name[0] in "qk" else 1
                if name == "q_0":
                    ps.wait_filled(pool, "y1.1.1")
                    pool.dma_start(CST2, late_in).then_inc(late_got, 16)
                    pool.memset(HB[:, :, 0:CONF_TAPS - 1], 0.0).then_inc(late_set, 1)
                    pool.memset(SB[:, :, 0:SC_TAPS - 1], 0.0).then_inc(late_set, 1)
                pool.wait_ge(means, n + 1)
                pool.tensor_tensor(RS[:, n, 0:w], MS[:, n, 0:w], HALFNEG[:, 0:w], ALU.pow).then_inc(rstds, 1)

        @block.scalar
        def _(act):
            do = Order(act, act_step)
            made, fence = [0], [FENCES["start"]]

            def feed(name, more=0):
                highs(first_split(name) + SPLIT_RING + more)

            def highs(upto):
                for s in range(made[0], min(upto, fence[0])):
                    n = split_pieces[s]
                    name, half, kb, width, _ = pieces[n]
                    if s >= SPLIT_RING:
                        act.wait_ge(*readers[split_pieces[s - SPLIT_RING]])
                    wait_raw(act, name, half)
                    do(act.activation(WH[:, s % SPLIT_RING, 0:kb * width], RAW[:, slot[n] % RAW_RING, 0:kb * width], ACT.Copy),
                       high_done)
                    made[0] = s + 1

            def square(name, t):
                do.after()
                scratch = GT[:, 16:24, :] if name == "n0" else ZS
                do(act.activation(scratch[:, 4 * t:4 * t + 4, :], X[:, t, :].rearrange("p (k s) -> p k s", k=4), ACT.Square,
                                  accum_out=SQ[:, powers.index(f"{name}_{t}"):powers.index(f"{name}_{t}") + 1]), squares)

            def evict_norm(n):
                for t in range(NT):
                    seen = 4 * n + 2 * t
                    bank = ps.wait_filled(act, f"n{n}.{t}.1")
                    if t:
                        act.wait_ge(ht_low, seen)
                    for j in range(4):
                        b = 4 + j
                        scale = MOD[:, b:b + 1] if n < 2 else col("mixg" if n == 2 else "ffng")[:, b:b + 1]
                        shift = ADA[:, b:b + 1] if n < 2 else 0.0
                        ins = act.activation(ROT2[:, j * P:(j + 1) * P], bank[:, j * P:(j + 1) * P], ACT.Identity,
                                             scale=scale, bias=shift)
                        if j < 3:
                            do(ins)
                        else:
                            ps.drain(ins, f"n{n}.{t}.1")
                    ps.wait_drained(act, f"n{n}.{t}.0")
                    do(act.activation(HH[:, 0:4, t * P:(t + 1) * P], ROT1[:, :].rearrange("p (b s) -> p b s", b=4), ACT.Copy),
                       ht_high)
                    ps.wait_drained(act, f"n{n}.{t}.1")
                    do(act.activation(HH[:, 4:8, t * P:(t + 1) * P], ROT2[:, :].rearrange("p (b s) -> p b s", b=4), ACT.Copy),
                       ht_high)

            def evict(use, dst, src=None, scale=1.0):
                bank = ps.wait_filled(act, use)
                src = bank[:, :] if src is None else src(bank)
                ps.drain(act.activation(dst, src, ACT.Copy, scale=scale), use)

            def flat4(bank):
                return bank[:, :].rearrange("p (b s) -> p b s", b=4)

            def flat2(bank):
                return bank[:, :].rearrange("p (b s) -> p b s", b=2)

            def head_turn(name, t):
                feed(name, 2 + t)
                i = rot_index[(name, t)]
                dst = KT if name[0] == "k" else QT
                base = 4 if name == "qb" or name.endswith("_1") else 0
                evict(f"{name}.{t}.T", dst[:, base:base + 4, t * P:(t + 1) * P], flat4)

            def gate_half(use, j):
                feed(use[:-2], int(use[-1]))
                evict(use, ZS[:, 2 * j:2 * j + 2, :], flat2, scale=0.5)
                if gates_made[0] >= 2:
                    act.wait_ge(gated, gates_made[0] - 1)
                ps.wait_drained(act, use)
                do(act.activation(ZT[:, gates_made[0] % 2, :].rearrange("p (b s) -> p b s", b=2), ZS[:, 2 * j:2 * j + 2, :],
                                  ACT.Tanh), tanh_done)
                gates_made[0] += 1

            gates_made = [0]

            def exps(u):
                x = units[u]
                if u >= 3:
                    ps.wait_filled(act, f"pt.{u - 3}")
                ps.wait_drained(act, f"s.{u}")
                if x["sink"] is not None:
                    h = x["sink"]
                    act.wait_ge(masked, h + 1)
                    do(act.activation(ES[:, h, :], NM[:, u, :], ACT.Exp, bias=SINK[:, h:h + 1]))
                do(act.activation(PR[:, u % 3, 0:P], E[:, u % 2, 0:P], ACT.Exp, scale=-1.0, bias=NM[:, u, 0:1],
                                  accum_out=DEN[:, u, 0:1]))
                do(act.activation(PR[:, u % 3, P:TRI], E[:, u % 2, P:TRI], ACT.Exp, scale=-1.0, bias=NM[:, u, 1:2],
                                  accum_out=DEN[:, u, 1:2]), exp_done)

            def probs_copy(u):
                ps.wait_filled(act, f"pt.{u}")
                if u >= 2:
                    if pv_at[u - 2] is None:
                        x = units[u - 2]
                        ps.wait_filled(act, f"o{0 if u - 2 < spans[0][1] else 1}.{x['o']}")
                    else:
                        act.wait_ge(pv_done, pv_at[u - 2])
                evict(f"pt.{u}", PT[:, u % 2, :], lambda bank: bank[:, 0:TRI])

            def high_heads(layer, o):
                if o == 0:
                    ps.wait_filled(act, ("zb.1", "z1_1.1")[layer])
                ps.wait_drained(act, f"o{layer}.{o}")
                do(act.activation(HH[:, o, :], ZS[:, o, :], ACT.Copy), ot_high)

            def attention(layer, extra):
                a, b = spans[layer]
                for i in range(a, b + 5):
                    if i < b:
                        exps(i)
                    if a <= i - 2 < b:
                        probs_copy(i - 2)
                    for what in extra.get(i - a, ()):
                        what()
                    for o in range(KB):
                        if high_step(layer, o) == i - a:
                            high_heads(layer, o)

            act.dma_start(X[:, :, :], x_in[0].rearrange("(t p) d -> p t d", t=NT)).then_inc(x_got, 16)
            act.wait_ge(cact_half, 1)
            do(act.activation(CACT[:, :], CTMP[:, :], ACT.Tanh), cact_tanh)
            act.wait_ge(x_got, 16)
            for t in range(NT):
                square("n0", t)
            feed("kcks", -2)
            act.wait_ge(mod_ready, 1)
            evict_norm(0)

            def values_out(t):
                feed("kcks", t)
                bank = ps.wait_filled(act, f"kcks.{t}")
                do(act.activation(VCD[:, t, :, :, :], bank[:, 256:384].rearrange("p (g d) -> p g d", g=2).unsqueeze(2)
                                  .to_broadcast([P, 2, 2, HD]), ACT.Copy))
                do(act.activation(V[:, t, 0:P], bank[:, 384:512], ACT.Copy), v_copied)

            def values_out2(t):
                feed("kakw", t)
                bank = ps.wait_filled(act, f"kakw.{t}")
                do(act.activation(V[:, t, P:P + 192], bank[:, 192:384], ACT.Copy))
                do(act.activation(G3[:, t, :], bank[:, 384:408], ACT.Tanh, scale=0.5), v_copied)

            def pair_out(t):
                bank = ps.wait_filled(act, f"up.{t}")
                v = bank[:, :].rearrange("p (b i l) -> p b i l", b=4, l=2)
                do(act.activation(UP[0:HD, :, t * 64:(t + 1) * 64], v[0:HD, :, :, 0], ACT.Copy))
                ps.drain(act.activation(UP[HD:P, :, t * 64:(t + 1) * 64], v[HD:P, :, :, 1], ACT.Copy), f"up.{t}")

            def keys_out(n):
                w = min(4, 10 - 4 * n)
                evict(f"kt.{n}", KT[:, 0:5, :].rearrange("p h (t s) -> p (h t) s", t=NT)[:, 4 * n:4 * n + w, :],
                      lambda bank: bank[:, 0:w * P].rearrange("p (b s) -> p b s", b=w))

            values_out(0)
            values_out(1)
            pair_out(0)
            values_out2(0)
            pair_out(1)
            values_out2(1)
            highs(FENCES["start"])
            for n in range(3):
                keys_out(n)
            head_turn("qa", 0)
            head_turn("qa", 1)
            head_turn("qb", 0)

            def hidden_tanh(kv):
                act.wait_ge(hid_in, kv + 1)
                do(act.activation(HTH[:, :], HQ[:, :], ACT.Tanh, scale=float(np.sqrt(2 / np.pi))), hid_tanh)

            hidden_tanh(0)
            head_turn("qb", 1)
            hidden_tanh(1)
            ps.wait_filled(act, "hid.1")
            fence[0] = FENCES["hidden"]
            feed("za")

            def gate_out():
                for c in range(2):
                    evict(f"gate0.{c}", GATE[:, c * 512:(c + 1) * 512])

            def compressed_out():
                evict("kc2", KCT[:, :, :], lambda bank: bank[:, 0:2 * NC].rearrange("p (g c) -> p g c", g=2))
                evict("vc2", VCM[:, :, :], lambda bank: bank[:, 0:P].rearrange("p (g d) -> p g d", g=2))

            def compressed_exp():
                act.wait_ge(cmp_masked, 1)
                do(act.activation(CE[:, :, :, :], CE[:, :, :, :], ACT.Exp, scale=SCALE), cmp_exp)

            attention(0, {0: [lambda: gate_half("za.0", 0)], 1: [lambda: gate_half("za.1", 1)], 3: [compressed_out],
                          6: [compressed_exp],
                          7: [gate_out], 8: [lambda: evict("cmpT", CPT[:, :, :], flat2), lambda: gate_half("zb.0", 2)],
                          10: [lambda: gate_half("zb.1", 3)], **past_columns(fence, highs, 14)})

            for t in range(NT):
                if t:
                    feed("wo0_0", 1)
                act.wait_ge(x_new, 2 * t + 2)
                square("n1", t)
            feed("wo0_1")
            act.wait_ge(mod_ready, 2)
            evict_norm(1)

            def values(name, t, base):
                feed(name, t)
                evict(f"{name}.{t}", V[:, t, base:base + 512])

            feed("q1_0")
            head_turn("q1_0", 0)
            head_turn("q1_0", 1)
            values("v1_0", 0, 0)
            head_turn("k1_0", 0)
            values("v1_0", 1, 0)
            head_turn("k1_0", 1)
            attention(1, {0: [lambda: gate_half("z1_0.0", 0)], 1: [lambda: gate_half("z1_0.1", 1)],
                          4: [lambda: head_turn("q1_1", 0)], 5: [lambda: head_turn("q1_1", 1)],
                          6: [lambda: values("v1_1", 0, 512), lambda: head_turn("k1_1", 0)],
                          7: [lambda: values("v1_1", 1, 512), lambda: head_turn("k1_1", 1)],
                          2: [lambda: feed("q1_1", 0)], 3: [lambda: feed("q1_1", 1)],
                          9: [lambda: gate_half("z1_1.0", 2)], 11: [lambda: gate_half("z1_1.1", 3)],
                          13: [lambda: feed("wo1_0")]})

            for c in range(2):
                evict(f"gate1.{c}", GATE[:, c * 512:(c + 1) * 512])

            for t in range(NT):
                if t:
                    feed("wo1_0", 1)
                act.wait_ge(x_new, 4 + 3 * t + 2)
                square("nf", t)
                act.wait_ge(x_new, 4 + 3 * t + 3)
                square("n2", t)
            feed("wo1_1")
            evict_norm(2)
            for j in range(2):
                feed("val", j)
                evict(f"val.{j}", VALH[:, 2 * j:2 * j + 2, :], flat2, scale=0.5)
            for j in range(2):
                feed("cga", j)
                bank = ps.wait_filled(act, f"cga.{j}")
                ps.drain(act.activation(ZT[:, j, :], bank[:, :], ACT.Tanh, scale=0.5), f"cga.{j}")

            def qk_square(name, t):
                i = 2 * (name == "k2") + t
                feed(name, t)
                bank = ps.wait_filled(act, f"{name}.{t}")
                if i >= 2:
                    ps.wait_drained(act, f"{'q2'}.{t}")
                do(act.activation(LNH[:, i % 2, :], bank[:, :], ACT.Square), qk_sq)

            def qk_turn(name, t):
                use = f"{name}.{t}.T"
                bank = ps.wait_filled(act, use)
                dst = QT if name == "q2" else KT
                g = 0 if name == "q2" else 1
                ps.drain(act.activation(dst[:, 0:4, t * P:(t + 1) * P], flat4(bank), ACT.Identity,
                                        scale=QKG[:, g:g + 1]), use)

            act.wait_ge(half_cols, 1)
            qk_square("q2", 0)
            qk_square("q2", 1)
            qk_turn("q2", 0)
            qk_square("k2", 0)
            qk_turn("q2", 1)
            qk_square("k2", 1)
            qk_turn("k2", 0)
            feed("v2")
            evict("v2.0", V[:, 0, 0:512])
            qk_turn("k2", 1)
            feed("v2", 1)
            evict("v2.1", V[:, 1, 0:512])
            for j in range(2):
                feed("scx", j)
                evict(f"scx.{j}", SCX[:, 2 * j:2 * j + 2, :], flat2)
            for name in ("scg", "sbg"):
                for j in range(2):
                    feed(name, j)
            for g in range(6):
                for j in range(2):
                    use = f"g{g}.{j}"
                    feed(f"g{g}", j)
                    bank = ps.wait_filled(act, use)
                    for b in range(2):
                        f = 4 * g + 2 * j + b
                        ins = act.activation(GT[:, f, :], bank[:, b * S:(b + 1) * S], ACT.Tanh, scale=0.5,
                                             bias=GBH[:, f:f + 1])
                        if b == 0:
                            do(ins)
                        else:
                            ps.drain(ins, use)
            highs(first_split("fi0"))
            for t in range(NT):
                use = f"lnT.{t}"
                bank = ps.wait_filled(act, use)
                for b in range(CB):
                    ins = act.activation(LNY[:, b, t * P:(t + 1) * P], bank[:, b * P:(b + 1) * P], ACT.Identity,
                                         scale=LGH[:, b:b + 1], bias=LBH[:, b:b + 1])
                    if b < CB - 1:
                        do(ins)
                    else:
                        ps.drain(ins, use)
                ps.wait_drained(act, use)
                do(act.activation(ZT[:, t, :].rearrange("p (b s) -> p b s", b=CB), LNY[:, :, t * P:(t + 1) * P], ACT.Tanh),
                   ln_tanh)

            def softplus_log(h):
                bank = ps.wait_filled(act, f"z.{h}")
                b = PR[:, h % 3, :]
                if h >= 3:
                    act.wait_ge(stick_p, h - 2)
                do(act.activation(b, bank[:, 0:TRI], ACT.Abs))
                do.after()
                do(act.activation(b, b, ACT.Exp, scale=-1.0))
                do.after()
                do(act.activation(b, b, ACT.Ln, bias=1.0), soft_ln)

            def stick_exp(h):
                ps.wait_drained(act, f"r.{h}")
                if h >= 2:
                    if h % 2:
                        ps.wait_filled(act, f"so.{(h - 2) // 2}")
                    else:
                        act.wait_ge(pv_done, stick_pv_at[h - 2])
                do(act.activation(PT[:, h % 2, :], PR[:, h % 3, :], ACT.Exp), stick_p)

            for i in range(S_HEADS + 2):
                if i < S_HEADS:
                    softplus_log(i)
                if 0 <= i - 2 < S_HEADS:
                    stick_exp(i - 2)
            fence[0] = FENCES["branches"]
            for j in range(4):
                act.wait_ge(merged, j + 1)
                do(act.activation(HH[:, 2 * j:2 * j + 2, :], merged_block(j), ACT.Copy), mt_high)
            for t in range(NT):
                if t:
                    feed("wf0", 1)
                for c in range(2):
                    ps.wait_drained(act, f"y2.{t}.{c}")
                square("n3", t)
            feed("wf1")
            evict_norm(3)

            def high_hidden(i):
                ps.wait_drained(act, f"fu.{i}")
                do(act.activation(AH[:, 2 * i:2 * i + 2, :], (ROT1, ROT2)[i % 2][:, :].rearrange("p (b s) -> p b s", b=2),
                                  ACT.Copy), ff_high)

            for i in range(FB // 2):
                feed(f"fi{i}")
                if i >= 2:
                    ps.wait_drained(act, f"fu.{i - 2}")
                bank = ps.wait_filled(act, f"fg.{i}")
                ps.drain(act.activation(ZT[:, i % 2, :], bank[:, :], ACT.Silu), f"fg.{i}")
                feed(f"fi{i}", 1)
                if i:
                    high_hidden(i - 1)
            high_hidden(FB // 2 - 1)
            highs(len(split))

        @block.vector
        def _(dve):
            do = Order(dve, dve_step)
            made, fence, behind = [0], [FENCES["start"]], [1]

            def feed(name, more=0):
                lows(first_split(name) + SPLIT_RING - behind[0] + more)

            def lows(upto):
                upto = min(upto, fence[0])
                stream(split_pieces[upto - 1] + 1)

            def stream(upto):
                for n in range(made[0], upto):
                    name, half, kb, width, use = pieces[n]
                    if use == "ada" and (name, half) in ada_pieces:
                        ada(name, half)
                    elif n in split:
                        s = split[n]
                        dve.wait_ge(high_done, s + 1)
                        w = slice(0, kb * width)
                        do(dve.tensor_tensor(WL[:, s % SPLIT_RING, w], RAW[:, slot[n] % RAW_RING, w], WH[:, s % SPLIT_RING, w],
                                             ALU.subtract), low_done)
                    made[0] = n + 1

            def ada(name, half):
                layer, c = int(name[3]), int(name[5])
                w = raw(name, half)
                wait_raw(dve, name, half)
                dve.wait_ge(bias_in, 16 * (layer + 1))
                acc = ACC[:, c * 512:(c + 1) * 512]
                for k in range(KB // 2):
                    kk = half * KB // 2 + k
                    do.after()
                    do(dve.scalar_tensor_tensor(acc, w[:, k, :], CACT[:, kk:kk + 1], acc, ALU.mult, ALU.add),
                       ada_read if k == KB // 2 - 1 else None)

            sq_seen = [0]

            def stat(name, t):
                i = powers.index(f"{name}_{t}")
                sq_seen[0] += 1
                dve.wait_ge(squares, sq_seen[0])
                do(dve.tensor_scalar(MS[:, i, 0:1], SQ[:, i:i + 1], 1.0 / D, EPS, ALU.mult, ALU.add), means)

            def hat(name, t):
                i = powers.index(f"{name}_{t}")
                dve.wait_ge(rstds, i + 1)
                do(dve.tensor_scalar(XH[:, t, :], X[:, t, :], RS[:, i, 0:1], None, ALU.mult), x_hat)

            def row_in(layer, c):
                use = f"cols{layer}.{c}"
                bank = ps.wait_filled(dve, use)
                dve.wait_ge(bias_in, 16 * (layer + 1))
                acc = ACC[0:1, c * 512:(c + 1) * 512]
                ps.drain(dve.tensor_tensor(acc, acc, bank[0:1, :], ALU.add), use)

            def modulation(layer):
                bank = ps.wait_filled(dve, f"ada{layer}")
                ps.drain(dve.tensor_copy(ADA[:, :], bank[:, 0:2 * KB]), f"ada{layer}")
                ps.wait_drained(dve, f"ada{layer}")
                do(dve.scalar_tensor_tensor(MOD[:, :], ADA[:, KB:2 * KB], 1.0, col(f"ng{layer}"), ALU.add, ALU.mult),
                   mod_ready)
                do.after()

            def evict_norm(n):
                for t in range(NT):
                    use = f"n{n}.{t}.0"
                    bank = ps.wait_filled(dve, use)
                    do.after()
                    for b in range(4):
                        dst, src = ROT1[:, b * P:(b + 1) * P], bank[:, b * P:(b + 1) * P]
                        if n < 2:
                            ins = dve.tensor_scalar(dst, src, MOD[:, b:b + 1], ADA[:, b:b + 1], ALU.mult, ALU.add)
                        else:
                            g = col("mixg" if n == 2 else "ffng")
                            ins = dve.tensor_scalar(dst, src, g[:, b:b + 1], None, ALU.mult)
                        if b < 3:
                            do(ins)
                        else:
                            ps.drain(ins, use)
                    for half, full in enumerate((ROT1, ROT2)):
                        dve.wait_ge(ht_high, 4 * n + 2 * t + half + 1)
                        at = (slice(None), slice(4 * half, 4 * half + 4), slice(t * P, (t + 1) * P))
                        do(dve.tensor_tensor(HL[at], full[:, :].rearrange("p (b s) -> p b s", b=4), HH[at], ALU.subtract),
                           ht_low)

            def rotate(name, t):
                i = rot_index[(name, t)]
                use = f"{name}.{t}"
                feed(name, t)
                heads = {"kcks": 4, "kakw": 3}.get(name, 8)
                bank = ps.wait_filled(dve, use)
                x = bank[:, 0:heads * HD].rearrange("p (h u d) -> p h u d", u=2, d=HALF)
                x3 = bank[:, 0:heads * HD].rearrange("p (h d) -> p h d", d=HD)
                c = const("ropec")[:, t * HD:(t + 1) * HD].unsqueeze(1).to_broadcast([P, heads, HD])
                s0 = const("ropes")[:, t * HD:t * HD + HALF].unsqueeze(1).to_broadcast([P, heads, HALF])
                s1 = const("ropes")[:, t * HD + HALF:(t + 1) * HD].unsqueeze(1).to_broadcast([P, heads, HALF])
                r1 = ROT1[:, 0:heads * HD].rearrange("p (h d) -> p h d", d=HD)
                r2 = ROT2[:, 0:heads * HD].rearrange("p (h u d) -> p h u d", u=2, d=HALF)
                if heads < 8:
                    dve.wait_ge(v_copied, i + 1)
                do.after()
                do(dve.tensor_tensor(r1, x3, c, ALU.mult))
                do(dve.tensor_tensor(r2[:, :, 0, :], x[:, :, 1, :], s0, ALU.mult))
                ps.drain(dve.tensor_tensor(r2[:, :, 1, :], x[:, :, 0, :], s1, ALU.mult), use)
                ps.wait_drained(dve, use)
                if heads < 8:
                    base = 0 if name == "kcks" else 4
                    a = ROT1[:, 0:heads * HD].rearrange("p (h d) -> p h d", d=HD).unsqueeze(2).to_broadcast([P, heads, 2, HD])
                    b = ROT2[:, 0:heads * HD].rearrange("p (h d) -> p h d", d=HD).unsqueeze(2).to_broadcast([P, heads, 2, HD])
                    dst = KR[:, t, base:base + heads, :].rearrange("p h (u d) -> p h u d", u=2)
                    do(dve.tensor_tensor(dst, a, b, ALU.add), roped)
                else:
                    if rot_order[i - 2][0] not in ("kcks", "kakw"):
                        n2, t2 = rot_order[i - 2]
                        ps.wait_filled(dve, f"{n2}.{t2}.T")
                    do(dve.tensor_tensor(QR[:, i % 2, :], ROT1[:, :], ROT2[:, :], ALU.add), roped)

            def build_u(kv):
                pe_ = col(("pek", "pev")[kv])
                for m in range(2):
                    src = UP[:, 2 * kv:2 * kv + 2, 8 * m:8 * m + 8 * NC].rearrange("p g (c j) -> p g j c", j=8)
                    emb = pe_[:, 8 * m:8 * m + 8].unsqueeze(1).unsqueeze(3).to_broadcast([P, 2, 8, NC])
                    do(dve.tensor_tensor(U[:, 2 * kv:2 * kv + 2, 8 * m:8 * m + 8, :], src, emb, ALU.add), u_built)

            def hidden(kv):
                bank = ps.wait_filled(dve, f"hid.{kv}")
                do.after()
                ps.drain(dve.tensor_copy(HX[:, :], bank[:, 0:4 * NC]), f"hid.{kv}")
                ps.wait_drained(dve, f"hid.{kv}")
                do(dve.tensor_tensor(HQ[:, :], HX[:, :], HX[:, :], ALU.mult))
                do.after()
                do(dve.tensor_scalar(HQ[:, :], HQ[:, :], 0.044715, 1.0, ALU.mult, ALU.add))
                do.after()
                do(dve.tensor_tensor(HQ[:, :], HQ[:, :], HX[:, :], ALU.mult), hid_in)
                do.after()
                do(dve.tensor_scalar(HX[:, :], HX[:, :], 0.5, None, ALU.mult))

            def hidden_out(kv):
                dve.wait_ge(hid_tanh, kv + 1)
                do.after()
                do(dve.scalar_tensor_tensor(HID[:, kv, :], HTH[:, :], 1.0, HX[:, :], ALU.add, ALU.mult),
                   hid_done if kv == 0 else None)
                if kv:
                    do.after()
                    dve.wait_ge(consts_set, 4)
                    for hb in range(2):
                        src = HID[:, 1, hb * 2 * NC:(hb + 1) * 2 * NC].rearrange("p (g c) -> p g c", g=2)
                        do(dve.tensor_copy(HID4[:, hb, :, :, 0:NC], src.unsqueeze(2).to_broadcast([P, 2, 4, NC])), hid_done)

            def mask_scores(u):
                x = units[u]
                bank = ps.wait_filled(dve, f"s.{u}")
                e = E[:, u % 2, :]
                m = const(x["mask"])
                do(dve.tensor_tensor_reduce(e[:, 0:P], bank[:, 0:P], m[:, 0:P], -SCALE, 3e38, ALU.add, ALU.min,
                                            NM[:, u, 0:1]))
                ps.drain(dve.tensor_tensor_reduce(e[:, P:TRI], bank[:, P:TRI], m[:, P:TRI], -SCALE, 3e38, ALU.add,
                                                  ALU.min, NM[:, u, 1:2]), f"s.{u}")
                if x["sink"] is not None:
                    ps.wait_drained(dve, f"s.{u}")
                    h = x["sink"]
                    do(dve.tensor_scalar(NM[:, u, :], NM[:, u, :], NSINK[:, h:h + 1], None, ALU.min), masked)

            def normalise(u):
                x = units[u]
                dve.wait_ge(exp_done, u + 1)
                den = DEN[:, u, :]
                if x["sink"] is not None:
                    do(dve.tensor_tensor(den, den, ES[:, x["sink"], :], ALU.add))
                    do.after()
                do(dve.reciprocal(den, den))
                do.after()
                if x["gate"] is not None:
                    do(dve.tensor_tensor(den, den, G3[:, :, x["gate"]], ALU.mult))
                    do.after()
                p = PR[:, u % 3, :]
                do(dve.tensor_scalar(p[:, 0:P], p[:, 0:P], DEN[:, u, 0:1], None, ALU.mult), probs)
                do(dve.tensor_scalar(p[:, P:TRI], p[:, P:TRI], DEN[:, u, 1:2], None, ALU.mult), probs)

            gates_made = [0]

            def gate(j):
                n = gates_made[0]
                dve.wait_ge(tanh_done, n + 1)
                z = ZS[:, 2 * j:2 * j + 2, :]
                do(dve.scalar_tensor_tensor(z, ZT[:, n % 2, :].rearrange("p (b s) -> p b s", b=2), 1.0, z, ALU.add,
                                            ALU.mult), gated)
                gates_made[0] += 1

            def heads_out(layer, u):
                x = units[u]
                if not (x["last"] and x["q"] % 2):
                    return
                use = f"o{layer}.{x['o']}"
                bank = ps.wait_filled(dve, use)
                do.after()
                dve.wait_ge(gated, 4 * layer + x["o"] // 2 + 1)
                z = ZS[:, x["o"], :]
                ps.drain(dve.tensor_tensor(z, bank[:, 0:S], z, ALU.mult), use)

            def low_heads(layer, o):
                dve.wait_ge(ot_high, KB * layer + o + 1)
                do(dve.tensor_tensor(HL[:, o, :], ZS[:, o, :], HH[:, o, :], ALU.subtract), ot_low)

            def attention(layer, extra):
                a, b = spans[layer]
                for i in range(a, b + 6):
                    if i < b:
                        mask_scores(i)
                    if a <= i - 1 < b:
                        normalise(i - 1)
                    for what in extra.get(i - a, ()):
                        what()
                    if a <= i - 4 < b:
                        heads_out(layer, i - 4)
                    for o in range(KB):
                        if high_step(layer, o) + 1 == i - a:
                            low_heads(layer, o)

            def add_output(layer):
                for t in range(NT):
                    for c in range(2):
                        use = f"y{layer}.{t}.{c}"
                        if (t, c) == (1, 0):
                            feed(f"wo{layer}_0", 1)
                        bank = ps.wait_filled(dve, use)
                        for cc in range(2):
                            ps.wait_drained(dve, f"gate{layer}.{cc}")
                        tmp = (ROT1, ROT2)[c]
                        do.after()
                        ps.drain(dve.tensor_tensor(tmp[:, :], bank[:, :], GATE[:, c * 512:(c + 1) * 512], ALU.mult), use)
                        ps.wait_drained(dve, use)
                        xs = X[:, t, c * 512:(c + 1) * 512]
                        do(dve.tensor_tensor(xs, xs, tmp[:, :], ALU.add), x_new)
                    if layer == 1:
                        stat("nf", t)
                        dve.wait_ge(fing_in, 16)
                        i = powers.index(f"nf_{t}")
                        dve.wait_ge(rstds, i + 1)
                        do(dve.scalar_tensor_tensor(X[:, t, :], X[:, t, :], RS[:, i, 0:1], FING[:, :], ALU.mult,
                                                    ALU.mult), x_new)
                        do.after()
                    stat(("n1", "n2")[layer], t)
                    hat(("n1", "n2")[layer], t)
                feed(f"wo{layer}_1")

            dve.wait_ge(cols_got, 16)
            do(dve.tensor_scalar(CTMP[:, :], col("c"), 0.5, None, ALU.mult), cact_half)
            dve.wait_ge(cact_tanh, 1)
            do(dve.scalar_tensor_tensor(CACT[:, :], CACT[:, :], 1.0, CTMP[:, :], ALU.add, ALU.mult), cact_ready)
            stream(index[("ada0_2", 0)])
            for t in range(NT):
                stat("n0", t)
            dve.wait_ge(x_got, 16)
            for t in range(NT):
                hat("n0", t)
            stream(index[("ada0_3", 1)])
            dve.wait_ge(sinks_got, 16)
            do(dve.tensor_scalar(NSINK[:, :], SINK[:, :], -1.0, None, ALU.mult))
            for tile, src, k in ((GBH, "gateb", 0.5), (LGH, "lng", 0.5), (LBH, "lnb", 0.5)):
                do(dve.tensor_scalar(tile[:, :], col(src), k, None, ALU.mult))
            do(dve.tensor_scalar(QKG[:, 0:1], col("qg"), SCALE, None, ALU.mult))
            do(dve.tensor_copy(QKG[:, 1:2], col("kg")), half_cols)
            row_in(0, 1)
            row_in(0, 3)
            dve.wait_ge(params_in, 16)
            modulation(0)
            feed("kcks", -2)
            evict_norm(0)
            rotate("kcks", 0)
            rotate("kcks", 1)
            rotate("kakw", 0)
            rotate("kakw", 1)
            lows(FENCES["start"])
            do(dve.tensor_scalar(G3[:, :, :], G3[:, :, :], 0.5, 0.5, ALU.mult, ALU.add))
            for t in range(NT):
                ps.wait_drained(dve, f"up.{t}")
            build_u(0)
            build_u(1)
            rotate("qa", 0)
            rotate("qa", 1)
            rotate("qb", 0)
            rotate("qb", 1)
            hidden(0)
            hidden_out(0)
            hidden(1)
            hidden_out(1)
            fence[0] = FENCES["hidden"]
            feed("za")

            def upto(name, half):
                return lambda: stream(index[(name, half)] + 1)

            def compressed_mask():
                m = const("cmpadd").rearrange("p (t c) -> p t c", t=NT).unsqueeze(2)
                m = m.to_broadcast([P, NT, B_HEADS // 2, NC])
                for half in range(2):
                    use = f"cmp.{half}"
                    bank = ps.wait_filled(dve, use)
                    s = bank[:, 0:NT * B_HEADS // 2 * NC].rearrange("p (t h c) -> p t h c", t=NT, h=B_HEADS // 2)
                    dst = CE[:, :, :, :].rearrange("p t (h u) c -> p t u h c", u=2)[:, :, half, :, :]
                    ps.drain(dve.tensor_tensor(dst, s, m, ALU.add), use)
                    ps.wait_drained(dve, use)
                do(dve.tensor_reduce(CM[:, 0, :, :], CE[:, :, :, :], AX.X, ALU.max))
                do.after()
                do(dve.tensor_tensor(CE[:, :, :, :], CE[:, :, :, :],
                                     CM[:, 0, :, :].unsqueeze(3).to_broadcast([P, NT, B_HEADS, NC]), ALU.subtract),
                   cmp_masked)

            def compressed_probs():
                dve.wait_ge(cmp_exp, 1)
                m = const("cmp01").rearrange("p (t c) -> p t c", t=NT).unsqueeze(2).to_broadcast([P, NT, B_HEADS, NC])
                do(dve.tensor_tensor(CE[:, :, :, :], CE[:, :, :, :], m, ALU.mult))
                do.after()
                do(dve.tensor_reduce(CM[:, 1, :, :], CE[:, :, :, :], AX.X, ALU.add))
                do.after()
                do(dve.tensor_tensor(CM[:, 1, :, :], CM[:, 1, :, :],
                                     const("cmpfix").unsqueeze(2).to_broadcast([P, NT, B_HEADS]), ALU.add))
                do.after()
                do(dve.reciprocal(CM[:, 2, :, :], CM[:, 1, :, :]))
                do.after()
                do(dve.tensor_tensor(CM[:, 3, :, :], CM[:, 2, :, :],
                                     G3[:, :, :].rearrange("p t (h b) -> p t h b", b=3)[:, :, :, 0], ALU.mult))
                do.after()
                dve.wait_ge(consts_set, 4)
                do(dve.tensor_tensor(CP[:, :, :, 0:NC], CE[:, :, :, :],
                                     CM[:, 3, :, :].unsqueeze(3).to_broadcast([P, NT, B_HEADS, NC]), ALU.mult), cmp_probs)

            attention(0, {1: [lambda: gate(0)], 2: [lambda: gate(1)], 6: [compressed_mask], 7: [compressed_probs],
                          9: [lambda: gate(2)], 10: [lambda: row_in(1, 1), upto("ada1_0", 0)],
                          11: [lambda: gate(3), upto("ada1_0", 1)], 13: [lambda: row_in(1, 3)],
                          14: [upto("ada1_2", 0)], 15: [upto("ada1_2", 1)], 3: [upto("ada0_4", 0)], 4: [upto("ada0_4", 1), upto("ada0_5", 0)],
                          5: [upto("ada0_5", 1)], **past_columns(fence, lows, 15)})
            add_output(0)

            modulation(1)
            evict_norm(1)
            for name, t in rot_order[8:12]:
                rotate(name, t)
            feed("v1_0")
            feed("v1_0", 1)
            attention(1, {0: [lambda: feed("z1_0")], 1: [lambda: feed("z1_0", 1), lambda: gate(0)],
                          6: [lambda: feed("v1_1")], 7: [lambda: feed("v1_1", 1)], 9: [lambda: feed("z1_1")],
                          11: [lambda: feed("z1_1", 1)], 13: [lambda: feed("wo1_0")], 14: [lambda: feed("wo1_0", 1)],
                          2: [lambda: gate(1), lambda: rotate("q1_1", 0)],
                          3: [lambda: rotate("q1_1", 1)], 4: [lambda: rotate("k1_1", 0)], 5: [lambda: rotate("k1_1", 1)],
                          10: [lambda: gate(2)], 12: [lambda: gate(3)]})
            add_output(1)
            behind[0] = 0

            evict_norm(2)
            dve.wait_ge(late_set, 2)
            feed("val")
            for j in range(2):
                feed("cga", j)
                ps.wait_drained(dve, f"val.{j}")
                ps.wait_drained(dve, f"cga.{j}")
                do(dve.scalar_tensor_tensor(HB[:, 2 * j:2 * j + 2, CONF_TAPS - 1:],
                                            ZT[:, j, :].rearrange("p (b s) -> p b s", b=2), 1.0,
                                            VALH[:, 2 * j:2 * j + 2, :], ALU.add, ALU.mult))
            do.after()
            taps = {}

            def conf_taps(lo, hi):
                w = col("confw")
                for k in range(lo, hi):
                    for b in range(CB):
                        wk = w[:, b * CONF_TAPS + k:b * CONF_TAPS + k + 1]
                        src = HB[:, b, k:k + S]
                        if k == 0:
                            ins = dve.tensor_scalar(CV[:, b, :], src, wk, col("confb")[:, b:b + 1], ALU.mult, ALU.add)
                        else:
                            do.after(taps[b])
                            ins = dve.scalar_tensor_tensor(CV[:, b, :], src, wk, CV[:, b, :], ALU.mult, ALU.add)
                        last = k == CONF_TAPS - 1 and b == CB - 1
                        taps[b] = do(ins, conv_done if last else None)

            def qk_norm(name, t):
                n = "q_" if name == "q2" else "k_"
                p = powers.index(f"{n}{t}")
                i = 2 * (name == "k2") + t
                use = f"{name}.{t}"
                feed(name, t)
                dve.wait_ge(qk_sq, i + 1)
                do(dve.tensor_reduce(MS[:, p, :], LNH[:, i % 2, :].rearrange("p (h d) -> p h d", h=S_HEADS), AX.X, ALU.add))
                do.after()
                do(dve.tensor_scalar(MS[:, p, :], MS[:, p, :], 1.0 / HD, EPS, ALU.mult, ALU.add), means)
                if name == "q2" or t >= 0:
                    conf_taps(*qk_pieces[i])
                bank = ps.wait_filled(dve, use)
                dve.wait_ge(rstds, p + 1)
                if i >= 2:
                    ps.wait_filled(dve, f"q2.{t}.T")
                ps.drain(dve.tensor_tensor(QR[:, i % 2, :].rearrange("p (h d) -> p h d", h=S_HEADS),
                                           bank[:, :].rearrange("p (h d) -> p h d", h=S_HEADS),
                                           RS[:, p, :].unsqueeze(2).to_broadcast([P, S_HEADS, HD]), ALU.mult), use)

            qk_pieces = [(0, 1), (1, 3), (3, 5), (5, 7)]
            for name in ("q2", "k2"):
                for t in range(NT):
                    qk_norm(name, t)
            feed("v2")
            conf_taps(7, 9)
            feed("v2", 1)
            conf_taps(9, 11)
            for j in range(2):
                feed("scx", j)
                conf_taps(11 + j, 12 + j)
            for j in range(2):
                feed("scg", j)
                bank = ps.wait_filled(dve, f"scg.{j}")
                ps.wait_drained(dve, f"scx.{j}")
                ps.drain(dve.tensor_tensor(SB[:, 2 * j:2 * j + 2, SC_TAPS - 1:],
                                           bank[:, :].rearrange("p (b s) -> p b s", b=2),
                                           SCX[:, 2 * j:2 * j + 2, :], ALU.mult), f"scg.{j}")
                ps.wait_drained(dve, f"scg.{j}")
            w = col("scw")
            for k in range(SC_TAPS):
                for b in range(CB):
                    wk = w[:, b * SC_TAPS + k:b * SC_TAPS + k + 1]
                    if k == 0:
                        ins = dve.tensor_scalar(SV[:, b, :], SB[:, b, k:k + S], wk, None, ALU.mult)
                    else:
                        do.after(taps[CB + b])
                        ins = dve.scalar_tensor_tensor(SV[:, b, :], SB[:, b, k:k + S], wk, SV[:, b, :], ALU.mult, ALU.add)
                    taps[CB + b] = do(ins)
            do.after()
            for j in range(2):
                feed("sbg", j)
                bank = ps.wait_filled(dve, f"sbg.{j}")
                sv = SV[:, 2 * j:2 * j + 2, :]
                ps.drain(dve.tensor_tensor(sv, bank[:, :].rearrange("p (b s) -> p b s", b=2), sv, ALU.mult), f"sbg.{j}")
            for n in range(12):
                feed(f"g{n // 2}", n % 2)
                conf_taps(13 + 2 * n, min(15 + 2 * n, CONF_TAPS))
            for t in range(NT):
                bank = ps.wait_filled(dve, f"ln.{t}")
                p = powers.index(f"ln_{t}")
                do(dve.bn_stats(STAT[:, t, 0:6], bank[:, :]))
                do.after()
                do(dve.bn_aggr(STAT[:, t, 6:8], STAT[:, t, 0:6]))
                do.after()
                do(dve.tensor_scalar(MS[:, p, 0:1], STAT[:, t, 7:8], EPS, None, ALU.add), means)
            for t in range(NT):
                p = powers.index(f"ln_{t}")
                dve.wait_ge(rstds, p + 1)
                ps.drain(dve.tensor_scalar(LNH[:, t, :], tiles[ps.uses[f"ln.{t}"][0]][:, :], STAT[:, t, 6:7],
                                           RS[:, p, 0:1], ALU.subtract, ALU.mult), f"ln.{t}")
            lows(first_split("fi0"))
            for t in range(NT):
                dve.wait_ge(ln_tanh, t + 1)
                y = LNY[:, :, t * P:(t + 1) * P]
                do(dve.scalar_tensor_tensor(y, ZT[:, t, :].rearrange("p (b s) -> p b s", b=CB), 1.0, y, ALU.add, ALU.mult),
                   ln_done)

            def branch(use, j, gate_block, first, last=False):
                bank = ps.wait_filled(dve, use)
                y = bank[:, :].rearrange("p (b s) -> p b s", b=2)
                g = GT[:, gate_block + 2 * j:gate_block + 2 * j + 2, :]
                m = merged_block(j)
                if first:
                    ps.drain(dve.scalar_tensor_tensor(m, g, 1.0, y, ALU.add, ALU.mult), use)
                    return
                tmp = (ROT1, ROT2)[j % 2][:, :].rearrange("p (b s) -> p b s", b=2)
                do.after()
                ps.drain(dve.scalar_tensor_tensor(tmp, g, 1.0, y, ALU.add, ALU.mult), use)
                ps.wait_drained(dve, use)
                do(dve.tensor_tensor(m, m, tmp, ALU.add), merged if last else None)

            def soft_mask(h):
                bank = ps.wait_filled(dve, f"z.{h}")
                dve.wait_ge(soft_ln, h + 1)
                if h >= 3:
                    ps.wait_filled(dve, f"r.{h - 3}")
                e, p = STICK[h % 3], PR[:, h % 3, :]
                do(dve.scalar_tensor_tensor(e, bank[:, 0:TRI], 0.0, p, ALU.max, ALU.add))
                do.after()
                do(dve.tensor_tensor(e, e, const("stick01"), ALU.mult), soft_masked)
                ps.drain(dve.tensor_tensor(p, bank[:, 0:TRI], const("stickadd"), ALU.add), f"z.{h}")

            def add_rest(h):
                bank = ps.wait_filled(dve, f"r.{h}")
                ps.wait_drained(dve, f"z.{h}")
                p = PR[:, h % 3, :]
                ps.drain(dve.tensor_tensor(p, bank[:, 0:TRI], p, ALU.add), f"r.{h}")

            for i in range(S_HEADS + 5):
                if i < S_HEADS:
                    soft_mask(i)
                if 0 <= i - 2 < S_HEADS:
                    add_rest(i - 2)
                if i < 4:
                    branch(f"sco.{i}", i, 16, True)
                elif i < 8:
                    branch(f"cfo.{i - 4}", i - 4, 8, False)
                if 0 <= i - 5 < S_HEADS and (i - 5) % 2:
                    o = (i - 5) // 2
                    bank = ps.wait_filled(dve, f"so.{o}")
                    ps.drain(dve.tensor_copy(OS[:, o, :], bank[:, 0:S]), f"so.{o}")
            fence[0] = FENCES["branches"]

            def low_merged(j):
                dve.wait_ge(mt_high, j + 1)
                do(dve.tensor_tensor(HL[:, 2 * j:2 * j + 2, :], merged_block(j), HH[:, 2 * j:2 * j + 2, :], ALU.subtract),
                   mt_low)

            for j in range(4):
                branch(f"ato.{j}", j, 0, False, True)
                low_merged(j)
            for t in range(NT):
                for c in range(2):
                    if (t, c) == (1, 0):
                        feed("wf0", 1)
                    use = f"y2.{t}.{c}"
                    bank = ps.wait_filled(dve, use)
                    xs = X[:, t, c * 512:(c + 1) * 512]
                    ps.drain(dve.scalar_tensor_tensor(xs, bank[:, :], 0.5, xs, ALU.mult, ALU.add), use)
                for c in range(2):
                    ps.wait_drained(dve, f"y2.{t}.{c}")
                stat("n3", t)
                hat("n3", t)
            feed("wf1")
            evict_norm(3)

            def low_hidden(i):
                dve.wait_ge(ff_high, i + 1)
                do(dve.tensor_tensor(AL[:, 2 * i:2 * i + 2, :], (ROT1, ROT2)[i % 2][:, :].rearrange("p (b s) -> p b s", b=2),
                                     AH[:, 2 * i:2 * i + 2, :], ALU.subtract), ff_low)

            for i in range(FB // 2):
                feed(f"fi{i}")
                if i:
                    low_hidden(i - 1)
                ps.wait_drained(dve, f"fg.{i}")
                bank = ps.wait_filled(dve, f"fu.{i}")
                do.after()
                ps.drain(dve.tensor_tensor((ROT1, ROT2)[i % 2][:, :], ZT[:, i % 2, :], bank[:, :], ALU.mult), f"fu.{i}")
                feed(f"fi{i}", 1)
            low_hidden(FB // 2 - 1)
            lows(len(split))
            for n in range(2 * NT):
                bank = ps.wait_filled(dve, f"ff.{n}")
                xs = X[:, n // 2, (n % 2) * 512:(n % 2 + 1) * 512]
                ps.drain(dve.tensor_tensor(xs, bank[:, :], xs, ALU.add), f"ff.{n}")


def constants(late=False):
    table, n = const_table(late)
    out = np.zeros((P, n), np.float32)

    def put(name, a):
        at, w = table[name]
        out[:, at:at + w] = np.asarray(a, np.float32).reshape(P, w)

    p = np.arange(P)
    if late:
        put("tri", -(p[:, None] >= p[None, :]).astype(np.float32))
        put("negone", -np.ones((P, P)))
        before = np.concatenate([p[:, None] < np.arange(S)[None, :], p[:, None] < p[None, :]], 1)
        put("stick01", before)
        put("stickadd", np.where(before, 0.0, NEG))
        return out
    put("ident", np.eye(P))
    inv = (np.float32(10000.0) ** (-np.arange(0, HD, 2, dtype=np.float32) / np.float32(HD))).astype(np.float32)
    ang = np.arange(S, dtype=np.float32)[:, None] * inv[None, :]
    c, s = np.cos(ang), np.sin(ang)
    put("ropec", np.concatenate([c, c], 1).reshape(NT, P, HD).transpose(1, 0, 2))
    put("ropes", np.concatenate([-s, s], 1).reshape(NT, P, HD).transpose(1, 0, 2))
    diff = np.concatenate([p[:, None] - p[None, :], P + p[:, None] - np.arange(S)[None, :]], 1)
    put("maskc", np.where(diff >= 0, 0.0, NEG))
    put("maskw", np.where((diff >= 0) & (diff < 128), 0.0, NEG))
    tok = np.arange(S).reshape(NT, P).T[:, :, None]
    reach = tok >= CMP_STRIDE * np.arange(NC)[None, None, :] + CMP_LEN - 1
    put("cmpadd", np.where(reach, 0.0, NEG))
    put("cmp01", reach)
    put("cmpfix", ~reach.any(2))
    return out


def kernel(**inputs):
    import concourse.bacc as _bacc
    from concourse.bass_utils import run_bass_kernel_spmd as _run

    a = {k: np.asarray(v) for k, v in inputs.items()}
    we = a["w_in_even"][0]
    off = np.cumsum([0, 512, 64, 64, 512, 512, 128, 128, 128, 128, 128, 128, 24, 512])
    qa, ka, va, za, qb, kc, vc, ks, vs, kw, vw, gb, zb = (we[:, off[i]:off[i + 1]] for i in range(13))
    wo = a["w_in_odd"][0]
    w2 = a["w_in_2"][0]
    wi = a["w_ffn_in_2"][0]
    named = {"kcks": np.concatenate([kc, ks, vc, vs], 1), "kakw": np.concatenate([ka, kw, va, vw, gb], 1),
             "qa": qa, "qb": qb, "za": za, "zb": zb, "w1k": a["cmp_w1_k"][0], "w1v": a["cmp_w1_v"][0],
             "q2": w2[:, 0:512], "k2": w2[:, 512:1024], "v2": w2[:, 1024:1536], "val": w2[:, 1536:2048],
             "cga": w2[:, 2048:2560], "scx": w2[:, 2560:3072], "sbg": w2[:, 3072:3584], "scg": w2[:, 3584:4096],
             "sco": a["w_sc_out_2"][0], "cfo": a["w_conf_out_2"][0], "ato": a["w_attn_out_2"][0]}
    for c in range(6):
        named[f"ada0_{c}"] = a["w_ada"][0][:, c * 512:(c + 1) * 512]
        named[f"ada1_{c}"] = a["w_ada"][1][:, c * 512:(c + 1) * 512]
        named[f"g{c}"] = w2[:, 4096 + c * 512:4096 + (c + 1) * 512]
    for c in range(2):
        cc = slice(c * 512, (c + 1) * 512)
        named[f"wo0_{c}"], named[f"wo1_{c}"] = a["w_out_even"][0][:, cc], a["w_out_odd"][0][:, cc]
        named[f"wf{c}"] = a["w_o_2"][0][:, cc]
        for i, n in enumerate("qkvz"):
            named[f"{n}1_{c}"] = wo[:, i * D + c * 512:i * D + (c + 1) * 512]
    for i in range(FB // 2):
        named[f"fi{i}"] = np.concatenate([wi[:, i * 256:(i + 1) * 256], wi[:, D_FF + i * 256:D_FF + (i + 1) * 256]], 1)
    for i in range((FB + 3) // 4):
        named[f"fo{i}"] = a["w_ffn_out_2"][0][i * 512:(i + 1) * 512]
    pieces = piece_table()
    weights = np.zeros((len(pieces), P, PIECE), np.float32)
    for n, (name, half, kb, width, use) in enumerate(pieces):
        w = named[name]
        by_columns = use == "cols" or name in ("sco", "cfo", "ato")
        w = w[:, half * width:(half + 1) * width] if by_columns else w[half * kb * P:(half + 1) * kb * P]
        weights[n, :, 0:kb * width] = w.reshape(kb, P, width).transpose(1, 0, 2).reshape(P, kb * width)

    def rows(v, n):
        return v.reshape(n, P).T

    def channels(w):
        return w.reshape(w.shape[0], CB, P).transpose(2, 1, 0).reshape(P, -1)

    def pairs(e):
        return e.reshape(16, P).T

    def twice(v):
        return np.concatenate([v, v]).reshape(P, 1)

    w2k = a["cmp_w2_k"][0].reshape(2, P, HD).transpose(1, 0, 2)
    w2v = a["cmp_w2_v"][0].reshape(2, P, HD).transpose(1, 0, 2)
    col_parts = {"c": rows(a["c"][0], KB), "ng0": rows(a["norm_g"][0], KB), "ng1": rows(a["norm_g"][1], KB),
                 "mixg": rows(a["mix_norm_g_2"][0], KB), "ffng": rows(a["ffn_norm_g_2"][0], KB),
                 "gateb": rows(a["gate_b_2"][0].reshape(-1), 24), "confw": channels(a["conf_dw_w_2"][0]),
                 "confb": rows(a["conf_dw_b_2"][0], CB), "lng": rows(a["conf_ln_g_2"][0], CB),
                 "lnb": rows(a["conf_ln_b_2"][0], CB), "scw": channels(a["sc_conv_w_2"][0]),
                 "qg": twice(a["q_norm_g_2"][0]), "kg": twice(a["k_norm_g_2"][0]), "pek": pairs(a["cmp_pe_k"][0]),
                 "pev": pairs(a["cmp_pe_v"][0])}
    w2 = np.concatenate([np.concatenate([w2k, w2k], 2).reshape(P, 256), w2v.reshape(P, 128)], 1)
    table, _ = column_table()
    cols = np.concatenate([col_parts[n] for n in table], 1)
    given = {"weights": weights, "x": a["x"], "consts": constants(), "late": constants(True), "cols": cols, "b_ada": a["b_ada"],
             "final_g": a["final_g"], "w2": w2, "sinks": a["a_sinks"][0]}
    nc = _bacc.Bacc("TRN2", target_bir_lowering=False, num_devices=1)
    arrays, args = {}, []
    for name, v in given.items():
        v = np.ascontiguousarray(v)
        arrays[f"in_{name}_dram"] = v
        args.append(nc.dram_tensor(f"in_{name}_dram", v.shape, mybir.dt.from_np(v.dtype), kind="ExternalInput").ap())
    args.append(nc.dram_tensor("out_0_dram", (1, S, D), F32, kind="ExternalOutput").ap())
    two_blocks_kernel(nc, *args)
    r = _run(nc, [arrays], core_ids=[0])
    return r.results[0]["out_0_dram"]
```
